# Optimizing a Trainium2 kernel written in Bass

```python
import jax, jax.numpy as jnp
from jax import lax
import numpy as np

D_MODEL = 1024
BATCH = 1
SEQ = 256
DEPTH = 2

CHUNK = 64
N_MIXERS = 2
POOL_WINDOWS = (2, 4, 8, 16)
POOL_GROUPS = len(POOL_WINDOWS)
POOL_GW = D_MODEL // POOL_GROUPS
N_HEADS = 16
HEAD_DIM = D_MODEL // N_HEADS
LEFT_CHUNKS = 8
BAND_CHUNKS = LEFT_CHUNKS + 1
BAND = BAND_CHUNKS * CHUNK
REL_CLIP = 256
D_FF = 2816
CONV_W = 3
N_A = (DEPTH + 1) // 2
N_B = DEPTH // 2
EPS = 1e-6


def rmsnorm(x, g):
    xf = x.astype(jnp.float32)
    y = xf * lax.rsqrt(jnp.mean(xf * xf, axis=-1, keepdims=True) + EPS)
    return (y * g.astype(jnp.float32)).astype(x.dtype)

def pool_mixer(h, w_pool, b_pool, scale):
    B, S, D = h.shape
    hf = h.astype(jnp.float32)
    csp = jnp.concatenate([jnp.zeros((B, 1, D), jnp.float32), jnp.cumsum(hf, axis=1)], axis=1)
    t = jnp.arange(S)
    outs = []
    for g, w in enumerate(POOL_WINDOWS):
        c = csp[:, :, g * POOL_GW:(g + 1) * POOL_GW]
        upper = c[:, 1:]
        lower = jnp.concatenate([jnp.zeros((B, w - 1, POOL_GW), jnp.float32), c[:, :S - w + 1]], axis=1)
        cnt = jnp.minimum(t + 1, w).astype(jnp.float32)[None, :, None]
        outs.append((upper - lower) / cnt)
    pooled = jnp.concatenate(outs, axis=-1)
    y = (pooled - hf).astype(h.dtype).reshape(B, S, POOL_GROUPS, POOL_GW)
    y = jnp.einsum('bsgc,gcd->bsgd', y, w_pool).reshape(B, S, D) + b_pool
    return y * scale

def head_rmsnorm(x, g):
    xf = x.astype(jnp.float32)
    y = xf * lax.rsqrt(jnp.mean(xf * xf, axis=-1, keepdims=True) + EPS)
    return (y * g.astype(jnp.float32)).astype(x.dtype)

def chunk_attention(h, w_qkv, q_norm, k_norm, rel_table, w_o):
    B, S, D = h.shape
    nc = S // CHUNK
    qkv = h @ w_qkv
    q, k, v = jnp.split(qkv, 3, axis=-1)
    q = head_rmsnorm(q.reshape(B, S, N_HEADS, HEAD_DIM), q_norm)
    k = head_rmsnorm(k.reshape(B, S, N_HEADS, HEAD_DIM), k_norm)
    v = v.reshape(B, S, N_HEADS, HEAD_DIM)
    q = q.reshape(B, nc, CHUNK, N_HEADS, HEAD_DIM)
    pad = jnp.zeros((B, LEFT_CHUNKS, CHUNK, N_HEADS, HEAD_DIM), k.dtype)
    kp = jnp.concatenate([pad, k.reshape(B, nc, CHUNK, N_HEADS, HEAD_DIM)], axis=1)
    vp = jnp.concatenate([pad, v.reshape(B, nc, CHUNK, N_HEADS, HEAD_DIM)], axis=1)
    rel = jnp.arange(CHUNK)[:, None] - jnp.arange(BAND)[None, :] + LEFT_CHUNKS * CHUNK
    idx = jnp.clip(rel, -REL_CLIP, REL_CLIP) + REL_CLIP
    bias = rel_table.astype(jnp.float32)[:, idx]
    band_chunk = jnp.repeat(jnp.arange(BAND_CHUNKS), CHUNK)
    scale = HEAD_DIM ** -0.5

    def one_chunk(c):
        qc = lax.dynamic_index_in_dim(q, c, axis=1, keepdims=False)
        kb = lax.dynamic_slice_in_dim(kp, c, BAND_CHUNKS, axis=1).reshape(B, BAND, N_HEADS, HEAD_DIM)
        vb = lax.dynamic_slice_in_dim(vp, c, BAND_CHUNKS, axis=1).reshape(B, BAND, N_HEADS, HEAD_DIM)
        s = jnp.einsum('bqhd,bkhd->bhqk', qc, kb).astype(jnp.float32) * scale + bias[None]
        valid = (band_chunk + c - LEFT_CHUNKS) >= 0
        s = jnp.where(valid[None, None, None, :], s, -1e30)
        p = jax.nn.softmax(s, axis=-1).astype(vb.dtype)
        return jnp.einsum('bhqk,bkhd->bqhd', p, vb)

    o = lax.map(one_chunk, jnp.arange(nc))
    o = jnp.transpose(o, (1, 0, 2, 3, 4)).reshape(B, S, D)
    return o @ w_o

def conv_ffn(h, w_gate, w_val, conv_w, conv_b, w_out):
    S = h.shape[1]
    a = h @ w_gate
    ap = jnp.pad(a, ((0, 0), (CONV_W - 1, 0), (0, 0)))
    a = ap[:, 0:S] * conv_w[0] + ap[:, 1:S + 1] * conv_w[1] + ap[:, 2:S + 2] * conv_w[2] + conv_b
    return (jax.nn.silu(a) * (h @ w_val)) @ w_out

def first_inputs(seed: int = 0) -> dict:
    key = jax.random.key(seed)
    ks = jax.random.split(key, 16)
    f32 = jnp.float32
    D, F = D_MODEL, D_FF
    nrm = lambda k, shape, s: jax.random.normal(k, shape, f32) * s
    return {
        "x": nrm(ks[0], (BATCH, SEQ, D), 1.0),
        "mix_norm": 1.0 + nrm(ks[1], (DEPTH, D), 0.02),
        "ffn_norm": 1.0 + nrm(ks[2], (DEPTH, D), 0.02),
        "pool_w": nrm(ks[3], (N_A, POOL_GROUPS, POOL_GW, POOL_GW), POOL_GW ** -0.5),
        "pool_b": nrm(ks[4], (N_A, D), 0.02),
        "pool_scale": 1.0 + nrm(ks[5], (N_A, D), 0.1),
        "attn_wqkv": nrm(ks[6], (N_B, D, 3 * D), D ** -0.5),
        "attn_q_norm": 1.0 + nrm(ks[7], (N_B, HEAD_DIM), 0.02),
        "attn_k_norm": 1.0 + nrm(ks[8], (N_B, HEAD_DIM), 0.02),
        "attn_rel_bias": nrm(ks[9], (N_B, N_HEADS, 2 * REL_CLIP + 1), 0.1),
        "attn_wo": nrm(ks[10], (N_B, D, D), D ** -0.5),
        "ffn_w_gate": nrm(ks[11], (DEPTH, D, F), D ** -0.5),
        "ffn_w_val": nrm(ks[12], (DEPTH, D, F), D ** -0.5),
        "ffn_conv_w": nrm(ks[13], (DEPTH, CONV_W, F), CONV_W ** -0.5),
        "ffn_conv_b": nrm(ks[14], (DEPTH, F), 0.02),
        "ffn_w_out": nrm(ks[15], (DEPTH, F, D), F ** -0.5),
    }

def first_block(x, mix_norm, ffn_norm, pool_w, pool_b, pool_scale, attn_wqkv, attn_q_norm,
              attn_k_norm, attn_rel_bias, attn_wo, ffn_w_gate, ffn_w_val, ffn_conv_w,
              ffn_conv_b, ffn_w_out):
    for i in range(DEPTH):
        h = rmsnorm(x, mix_norm[i])
        j = i // N_MIXERS
        if i % N_MIXERS == 0:
            x = x + pool_mixer(h, pool_w[j], pool_b[j], pool_scale[j])
        else:
            x = x + chunk_attention(h, attn_wqkv[j], attn_q_norm[j], attn_k_norm[j],
                                    attn_rel_bias[j], attn_wo[j])
        h = rmsnorm(x, ffn_norm[i])
        x = x + conv_ffn(h, ffn_w_gate[i], ffn_w_val[i], ffn_conv_w[i], ffn_conv_b[i], ffn_w_out[i])
    return x


DEPTH_2 = 1

RET_HEADS = 8
RET_DK = 64
RET_DV = 128
RET_CHUNK = 128
ROPE_BASE = 10000.0
SB_HEADS = 8
SB_DH = 64
SB_BLOCK = 128
PEER_HEADS = 8
N_KEYS = 128
N_EXPERTS = N_KEYS * N_KEYS
PEER_TOPK = 16
PEER_DKEY = 256
PEER_CHUNK = 128

RET_QK = RET_HEADS * RET_DK
RET_V = RET_HEADS * RET_DV
SB_W = SB_HEADS * SB_DH
IN_SIZES = (RET_QK, RET_QK, RET_V, RET_V, SB_W, SB_W, SB_W, D_MODEL, D_MODEL)
IN_WIDTH = sum(IN_SIZES)


def rmsnorm_2(x, g):
    xf = x.astype(jnp.float32)
    y = xf * lax.rsqrt(jnp.mean(xf * xf, axis=-1, keepdims=True) + EPS)
    return (y * g.astype(jnp.float32)).astype(x.dtype)

def group_norm(y, g):
    yf = y.astype(jnp.float32)
    mu = jnp.mean(yf, axis=-1, keepdims=True)
    var = jnp.mean(jnp.square(yf - mu), axis=-1, keepdims=True)
    return (yf - mu) * lax.rsqrt(var + EPS) * g.astype(jnp.float32)

def rope(x, pos):
    half = x.shape[-1] // 2
    freqs = ROPE_BASE ** (-jnp.arange(half, dtype=jnp.float32) / half)
    ang = pos[:, None] * freqs[None, :]
    cos = jnp.cos(ang)[:, None, :]
    sin = jnp.sin(ang)[:, None, :]
    xf = x.astype(jnp.float32)
    x1, x2 = xf[..., :half], xf[..., half:]
    return jnp.concatenate([x1 * cos - x2 * sin, x1 * sin + x2 * cos], axis=-1)

def retention(q, k, v):
    B, S, H, dk = q.shape
    dv = v.shape[-1]
    C = RET_CHUNK
    n = S // C
    log_g = jnp.log1p(-jnp.exp2(-5.0 - jnp.arange(H, dtype=jnp.float32)))
    i = jnp.arange(C, dtype=jnp.float32)
    diff = i[:, None] - i[None, :]
    dmask = jnp.where(diff >= 0, jnp.exp(log_g[:, None, None] * jnp.maximum(diff, 0.0)), 0.0)
    q_dec = jnp.exp(log_g[:, None] * (i + 1.0)).T[None, :, :, None]
    k_dec = jnp.exp(log_g[:, None] * (C - 1.0 - i)).T[None, :, :, None]
    c_dec = jnp.exp(log_g * C)[None, :, None, None]

    def chunks(t):
        return jnp.moveaxis(t.reshape(B, n, C, H, t.shape[-1]), 1, 0)

    def step(state, xs):
        qc, kc, vc = xs
        scores = jnp.einsum('bihd,bjhd->bhij', qc, kc) * dmask[None]
        y = jnp.einsum('bhij,bjhe->bihe', scores, vc)
        y = y + jnp.einsum('bihd,bhde->bihe', qc, state) * q_dec
        state = state * c_dec + jnp.einsum('bjhd,bjhe->bhde', kc * k_dec, vc)
        return state, y

    state0 = jnp.zeros((B, H, dk, dv), jnp.float32)
    _, ys = lax.scan(step, state0, (chunks(q), chunks(k), chunks(v)))
    return jnp.moveaxis(ys, 0, 1).reshape(B, S, H, dv)

def stick_breaking(q, k, v):
    B, S, H, d = q.shape
    n = S // SB_BLOCK
    scale = SB_DH ** -0.5
    qh = jnp.transpose(q, (0, 2, 1, 3))
    kh = jnp.transpose(k, (0, 2, 1, 3))
    vh = jnp.transpose(v, (0, 2, 1, 3))
    qb = jnp.moveaxis(qh.reshape(B, H, n, SB_BLOCK, d), 2, 0)
    kpos = jnp.arange(S)

    def block(args):
        qi, bi = args
        z = jnp.einsum('bhtd,bhsd->bhts', qi, kh).astype(jnp.float32) * scale
        tpos = bi * SB_BLOCK + jnp.arange(SB_BLOCK)
        mask = kpos[None, :] < tpos[:, None]
        log_stay = jnp.where(mask, jax.nn.log_sigmoid(-z), 0.0)
        later = lax.cumsum(log_stay, axis=3, reverse=True) - log_stay
        w = jnp.where(mask, jnp.exp(jax.nn.log_sigmoid(z) + later), 0.0)
        return jnp.einsum('bhts,bhsd->bhtd', w.astype(vh.dtype), vh)

    out = lax.map(block, (qb, jnp.arange(n)))
    out = jnp.moveaxis(out, 0, 2).reshape(B, H, S, d)
    return jnp.transpose(out, (0, 2, 1, 3)).reshape(B, S, H * d)

def peer(x, w_q, sub_keys_1, sub_keys_2, u_tab, v_tab):
    B, S, D = x.shape
    T = PEER_CHUNK
    n = S // T
    xc = jnp.moveaxis(x.reshape(B, n, T, D), 1, 0)
    k1 = sub_keys_1.astype(jnp.float32)
    k2 = sub_keys_2.astype(jnp.float32)

    def block(xb):
        q = (xb @ w_q).reshape(B, T, PEER_HEADS, 2, PEER_DKEY // 2).astype(jnp.float32)
        s1 = jnp.einsum('bthd,nd->bthn', q[..., 0, :], k1)
        s2 = jnp.einsum('bthd,nd->bthn', q[..., 1, :], k2)
        v1, i1 = lax.top_k(s1, PEER_TOPK)
        v2, i2 = lax.top_k(s2, PEER_TOPK)
        cand_s = (v1[..., :, None] + v2[..., None, :]).reshape(B, T, PEER_HEADS, PEER_TOPK * PEER_TOPK)
        cand_i = (i1[..., :, None] * N_KEYS + i2[..., None, :]).reshape(B, T, PEER_HEADS, PEER_TOPK * PEER_TOPK)
        top_s, pos = lax.top_k(cand_s, PEER_TOPK)
        idx = jnp.take_along_axis(cand_i, pos, axis=-1)
        g = jax.nn.softmax(top_s, axis=-1)
        u_sel = jnp.take(u_tab, idx, axis=0)
        h = jnp.einsum('bthkd,btd->bthk', u_sel, xb)
        a = (jax.nn.gelu(h.astype(jnp.float32)) * g).astype(xb.dtype)
        return jnp.einsum('bthk,bthkd->btd', a, jnp.take(v_tab, idx, axis=0))

    y = lax.map(block, xc)
    return jnp.moveaxis(y, 0, 1).reshape(B, S, D)

def second_inputs(seed: int = 0) -> dict:
    key = jax.random.key(seed)
    ks = jax.random.split(key, 17)
    f = jnp.float32
    nrm = lambda k, shape, s: jax.random.normal(k, shape, f) * s
    gain = lambda k, shape: 1.0 + 0.02 * jax.random.normal(k, shape, f)
    return {
        'x': jax.random.normal(ks[0], (BATCH, SEQ, D_MODEL), f),
        'norm_attn': gain(ks[1], (DEPTH_2, D_MODEL)),
        'w_in': nrm(ks[2], (DEPTH_2, D_MODEL, IN_WIDTH), D_MODEL ** -0.5),
        'ret_q_norm': gain(ks[3], (DEPTH_2, RET_DK)),
        'ret_k_norm': gain(ks[4], (DEPTH_2, RET_DK)),
        'ret_group_norm': gain(ks[5], (DEPTH_2, RET_V)),
        'sb_q_norm': gain(ks[6], (DEPTH_2, SB_DH)),
        'sb_k_norm': gain(ks[7], (DEPTH_2, SB_DH)),
        'w_branch_ret': nrm(ks[8], (DEPTH_2, RET_V, D_MODEL), RET_V ** -0.5),
        'w_branch_sb': nrm(ks[9], (DEPTH_2, SB_W, D_MODEL), SB_W ** -0.5),
        'w_out': nrm(ks[10], (DEPTH_2, D_MODEL, D_MODEL), D_MODEL ** -0.5),
        'norm_ffn': gain(ks[11], (DEPTH_2, D_MODEL)),
        'peer_w_q': nrm(ks[12], (DEPTH_2, D_MODEL, PEER_HEADS * PEER_DKEY), D_MODEL ** -0.5),
        'peer_sub_keys_1': nrm(ks[13], (DEPTH_2, N_KEYS, PEER_DKEY // 2), (PEER_DKEY // 2) ** -0.5),
        'peer_sub_keys_2': nrm(ks[14], (DEPTH_2, N_KEYS, PEER_DKEY // 2), (PEER_DKEY // 2) ** -0.5),
        'peer_u': nrm(ks[15], (DEPTH_2, N_EXPERTS, D_MODEL), D_MODEL ** -0.5),
        'peer_v': nrm(ks[16], (DEPTH_2, N_EXPERTS, D_MODEL), PEER_HEADS ** -0.5),
    }

def second_block(x, norm_attn, w_in, ret_q_norm, ret_k_norm, ret_group_norm, sb_q_norm, sb_k_norm,
              w_branch_ret, w_branch_sb, w_out, norm_ffn, peer_w_q, peer_sub_keys_1,
              peer_sub_keys_2, peer_u, peer_v):
    B, S, D = x.shape
    pos = jnp.arange(S, dtype=jnp.float32)
    split_points = np.cumsum(IN_SIZES)[:-1].tolist()
    for l in range(DEPTH_2):
        xn = rmsnorm_2(x, norm_attn[l])
        proj = xn @ w_in[l]
        rq, rk, rv, rg, sq, sk, sv, ga, gb = jnp.split(proj, split_points, axis=-1)

        rq = rope(rmsnorm_2(rq.reshape(B, S, RET_HEADS, RET_DK), ret_q_norm[l]), pos)
        rk = rope(rmsnorm_2(rk.reshape(B, S, RET_HEADS, RET_DK), ret_k_norm[l]), pos) * (RET_DK ** -0.5)
        ret = retention(rq, rk, rv.reshape(B, S, RET_HEADS, RET_DV).astype(jnp.float32))
        ret = group_norm(ret, ret_group_norm[l].reshape(RET_HEADS, RET_DV)).reshape(B, S, RET_V)
        ret = ret.astype(x.dtype) * jax.nn.silu(rg)
        y_a = ret @ w_branch_ret[l]

        sq = rmsnorm_2(sq.reshape(B, S, SB_HEADS, SB_DH), sb_q_norm[l])
        sk = rmsnorm_2(sk.reshape(B, S, SB_HEADS, SB_DH), sb_k_norm[l])
        sb = stick_breaking(sq, sk, sv.reshape(B, S, SB_HEADS, SB_DH))
        y_b = sb @ w_branch_sb[l]

        mixed = jax.nn.sigmoid(ga) * y_a + jax.nn.sigmoid(gb) * y_b
        x = x + mixed @ w_out[l]

        hn = rmsnorm_2(x, norm_ffn[l])
        x = x + peer(hn, peer_w_q[l], peer_sub_keys_1[l], peer_sub_keys_2[l], peer_u[l], peer_v[l])
    return x


def setup_inputs(seed=0):
    out = dict(first_inputs(seed))
    for name, value in second_inputs(seed + 1).items():
        if name != "x":
            out[name + "_2"] = value
    return out


def reference(
    x, mix_norm, ffn_norm, pool_w, pool_b, pool_scale, attn_wqkv, attn_q_norm, attn_k_norm,
    attn_rel_bias, attn_wo, ffn_w_gate, ffn_w_val, ffn_conv_w, ffn_conv_b, ffn_w_out,
    norm_attn_2, w_in_2, ret_q_norm_2, ret_k_norm_2, ret_group_norm_2, sb_q_norm_2, sb_k_norm_2,
    w_branch_ret_2, w_branch_sb_2, w_out_2, norm_ffn_2, peer_w_q_2, peer_sub_keys_1_2,
    peer_sub_keys_2_2, peer_u_2, peer_v_2,
):
    x = first_block(
        x, mix_norm, ffn_norm, pool_w, pool_b, pool_scale, attn_wqkv, attn_q_norm, attn_k_norm,
        attn_rel_bias, attn_wo, ffn_w_gate, ffn_w_val, ffn_conv_w, ffn_conv_b, ffn_w_out,
    )
    return second_block(
        x, norm_attn_2, w_in_2, ret_q_norm_2, ret_k_norm_2, ret_group_norm_2, sb_q_norm_2,
        sb_k_norm_2, w_branch_ret_2, w_branch_sb_2, w_out_2, norm_ffn_2, peer_w_q_2,
        peer_sub_keys_1_2, peer_sub_keys_2_2, peer_u_2, peer_v_2,
    )


_drawn_inputs = setup_inputs


def setup_inputs(seed=0):
    import zlib

    import numpy as np

    out = dict(_drawn_inputs(seed))
    spreads = {}
    factors = {'attn_q_norm': 8.0,
     'attn_k_norm': 8.0,
     'attn_rel_bias': 3.495,
     'ffn_conv_b': 3.16,
     'norm_attn_2': 3.824,
     'ret_q_norm_2': 7.126,
     'ret_k_norm_2': 7.228,
     'ret_group_norm_2': 20.917,
     'sb_q_norm_2': 32.76,
     'sb_k_norm_2': 30.467,
     'norm_ffn_2': 28.128}
    for name, (base, spread) in spreads.items():
        noise = np.random.default_rng([zlib.crc32(name.encode()), seed]).standard_normal(out[name].shape)
        drawn = base * np.exp(spread * noise) if base else spread * noise
        out[name] = __import__('jax').numpy.asarray(drawn.astype(out[name].dtype))
    for name, factor in factors.items():
        out[name] = (out[name] * factor).astype(out[name].dtype)
    return out
```

```python
import math
from contextlib import ExitStack

import numpy as np

import concourse.bass as bass
from concourse import mybir

F = mybir.dt.float32
R = mybir.dt.float32r
U32 = mybir.dt.uint32
ALU = mybir.AluOpType
ACT = mybir.ActivationFunctionType
AX = mybir.AxisListType.X

T = 256
D = 1024
KD = D // 128
FF = 2816
JF = FF // 128
EPS = 1e-6
NRAW = 4
NSPLIT = 3
BLK = 1024
N_POOL, N_FFN, N_ATT = 2, 3 * JF, 32
N_IN, N_BR, N_PQ = 52, 20, 16
N_BLOCKS = N_POOL + 2 * N_FFN + N_ATT + N_IN + N_BR + N_PQ + 256
NEG = -3.4028234663852886e38

_PARAMS = [("mix_norm0", 8), ("mix_norm1", 8), ("ffn_norm0", 8), ("ffn_norm1", 8), ("pool_b", 8),
           ("pool_scale", 8), ("attn_q_norm", 1), ("attn_k_norm", 1), ("conv0", 66), ("conv1", 66),
           ("conv_b0", 22), ("conv_b1", 22), ("norm_attn_2", 8), ("ret_q_norm", 1), ("ret_k_norm", 1),
           ("group_norm", 8), ("sb_q_norm", 1), ("sb_k_norm", 1), ("norm_ffn_2", 8)]
PCOL = {}
NPAR = 0
for _n, _w in _PARAMS:
    PCOL[_n] = NPAR
    NPAR += _w

_CONSTS = [("ident", 128), ("ones", 128), ("blk64", 128), ("rot", 128), ("tri", 128), ("iota", 128)]
CCOL = {}
NCON = 0
for _n, _w in _CONSTS:
    CCOL[_n] = NCON
    NCON += _w
LCOL = {"invcnt": (0, 1024), "decay": (1024, 3072), "cos": (4096, 256), "sin": (4352, 256), "nmask": (4608, 384)}
NLATE = 4992


class Queue:

    def __init__(self, sem):
        self.sem, self.count, self.items, self.seen = sem, 0, [], {}

    def wait(self, *toks):
        for t in toks:
            if t is None:
                continue
            if isinstance(t, list):
                self.wait(*t)
                continue
            sem, val = t
            if val and self.seen.get(sem.name, 0) < val:
                self.seen[sem.name] = val
                self.items.append(("w", sem, val))

    def do(self, fn, *toks, inc=True):
        self.wait(*toks)
        if inc:
            self.count += 1
        self.items.append(("i", fn, (self.sem, 1) if inc else None))
        return (self.sem, self.count)

    def dma(self, fn, chan, *toks):
        self.wait(*toks)
        chan[1] += 16
        self.items.append(("i", fn, (chan[0], 16)))
        return (chan[0], chan[1])

    @property
    def last(self):
        return (self.sem, self.count)

    def replay(self, eng):
        for kind, a, b in self.items:
            if kind == "w":
                eng.wait_ge(a, b)
            else:
                ins = a(eng)
                if b:
                    ins.then_inc(*b)


class Bank:
    def __init__(self, t):
        self.t, self.free = t, None


def build(nc, wall, par, con, late, xt, rev, keys, out, upto=99):
    ctx = ExitStack()
    with ctx:
        def sb(name, shape, dt=F):
            return ctx.enter_context(nc.sbuf_tensor(name, shape, dt))

        def sem(name):
            return ctx.enter_context(nc.semaphore(name))

        XT = sb("XT", [128, KD, T])
        HH = sb("HH", [128, KD, T], R)
        HL = sb("HL", [128, KD, T], R)
        GH = sb("GH", [128, 2, T], R)
        GL = sb("GL", [128, 2, T], R)
        RAW = sb("RAW", [128, NRAW, BLK])
        WH = sb("WH", [128, NSPLIT, BLK], R)
        WL = sb("WL", [128, NSPLIT, BLK], R)
        BIG = sb("BIG", [128, 32768])
        PAR = sb("PAR", [128, NPAR])
        CON = sb("CON", [128, NCON])
        RT = sb("RT", [128, 3, T])
        GS = sb("GS", [128, 2, T], R)
        EPSC = sb("EPSC", [128, 1])
        ONEC = sb("ONEC", [128, 1])
        banks = [Bank(ctx.enter_context(nc.psum_tensor(f"ps{i}", [128, 512], F))) for i in range(8)]

        PE, V, A, G, S = (Queue(sem(n)) for n in ("s_pe", "s_dve", "s_act", "s_pool", "s_sp"))
        c_par, c_con, c_late, c_x, c_rev, c_key, c_out = ([sem(n), 0] for n in (
            "d_par", "d_con", "d_late", "d_x", "d_rev", "d_key", "d_out"))
        c_raw = [[sem(f"d_raw{i}"), 0] for i in range(NRAW)]

        def par_col(name, j=0):
            c = PCOL[name] + j
            return PAR[:, c:c + 1]

        def con_of(name):
            return CON[:, CCOL[name]:CCOL[name] + 128]

        IDENT, ONES, BLK64, ROT, TRI, IOTA = (con_of(n) for n in ("ident", "ones", "blk64", "rot", "tri", "iota"))

        class Scratch:

            def __init__(self):
                self.at = 32768

            def take(self, n):
                self.at -= n
                assert self.at >= 0
                return BIG[:, self.at:self.at + n]

            def take3(self, m, n):
                return self.take(m * n).rearrange("p (m n) -> p m n", n=n)

        def mm(o, l, r, start, stop, *toks, inc=False):
            return PE.do(lambda e: e.matmul(o, l, r, start=start, stop=stop, skip_group_check=True), *toks, inc=inc)

        def act(o, i, f, *toks, bias=None, scale=None, accum=None):
            kw = {}
            if bias is not None:
                kw["bias"] = bias
            if scale is not None:
                kw["scale"] = scale
            if accum is not None:
                kw["accum_out"] = accum
            return A.do(lambda e: e.activation(o, i, f, **kw), *toks)

        def tt(o, a, b, op, *toks, q=None):
            return (q or V).do(lambda e: e.tensor_tensor(o, a, b, op), *toks)

        def ts(o, a, s1, s2, op0, op1, *toks):
            if op1 is None:
                return V.do(lambda e: e.tensor_scalar(o, a, s1, None, op0), *toks)
            return V.do(lambda e: e.tensor_scalar(o, a, s1, s2, op0, op1), *toks)

        def stt(o, a, s, b, op0, op1, *toks):
            return V.do(lambda e: e.scalar_tensor_tensor(out=o, in0=a, scalar=s, in1=b, op0=op0, op1=op1), *toks)

        def vcopy(o, a, *toks):
            return V.do(lambda e: e.tensor_copy(o, a), *toks)

        def recip(o, a, *toks):
            return V.do(lambda e: e.reciprocal(o, a), *toks)

        def split(src, hi, lo, ready, *frees):
            th = act(hi, src, ACT.Copy, ready, *frees)
            return tt(lo, src, hi.bitcast(F), ALU.subtract, th, ready, *frees)

        def sync_all():
            lasts = [q.last for q in (PE, V, A, G)]
            for q in (PE, V, A, G, S):
                q.wait(*lasts)

        class Weights:
            def __init__(self):
                self.loaded = self.splitted = self.taken = 0
                self.raw_free = [None] * NRAW
                self.free = [None] * NSPLIT
                self.raw_tok, self.tok = {}, {}

            def load(self):
                b = self.loaded
                if b >= N_BLOCKS:
                    return
                s = b % NRAW
                self.raw_tok[b] = S.dma(lambda e: e.dma_start(RAW[:, s, :], wall[b]), c_raw[s], self.raw_free[s])
                self.loaded += 1

            def split(self):
                b = self.splitted
                if b >= N_BLOCKS:
                    return
                r, s = b % NRAW, b % NSPLIT
                self.tok[b] = split(RAW[:, r, :], WH[:, s, :], WL[:, s, :], self.raw_tok[b], self.free[s])
                self.raw_free[r] = self.tok[b]
                self.splitted += 1
                self.load()

            def take(self):
                b = self.taken
                self.taken += 1
                s = b % NSPLIT
                return WH[:, s, :], WL[:, s, :], self.tok[b]

            def done(self, tok):
                self.free[(self.taken - 1) % NSPLIT] = tok
                self.split()

        W = Weights()
        ring = [0]

        def work():
            ring[0] += 1
            return banks[4 + ring[0] % 4]

        def mm3(o, lh, ll, rh, rl, first, last, *toks, inc=False):
            mm(o, lh, rh, first, False, *toks)
            mm(o, lh, rl, False, False)
            return mm(o, ll, rh, False, last, inc=inc)

        def c128(i):
            return slice(128 * i, 128 * i + 128)

        def project_t(nk, wtile, lhs_tok, hi, lo, h_tok):
            bank = work()
            for k in range(nk):
                wh, wl = wtile(k)
                tok = mm3(bank.t[:, 0:T], wh, wl, hi[:, k, :], lo[:, k, :], k == 0, k == nk - 1,
                          lhs_tok, h_tok, bank.free, inc=(k == nk - 1))
            return bank, tok

        def project_block(hi, lo, h_tok):
            wh, wl, wt = W.take()
            bank, tok = project_t(KD, lambda k: (wh[:, c128(k)], wl[:, c128(k)]), wt, hi, lo, h_tok)
            W.done(tok)
            return bank, tok

        def project_natural(hi, lo, h_tok, ncols):
            for c in range(ncols // 512):
                b2 = [work(), work()]
                for kb in range(4):
                    wh, wl, wt = W.take()
                    for tt_ in range(2):
                        for k2 in range(2):
                            k = 2 * kb + k2
                            tok = mm3(b2[tt_].t[:, :], hi[:, k, c128(tt_)], lo[:, k, c128(tt_)],
                                      wh[:, 512 * k2:512 * k2 + 512], wl[:, 512 * k2:512 * k2 + 512],
                                      k == 0, k == KD - 1, wt, h_tok, b2[tt_].free, inc=True)
                    W.done(tok)
                yield c, b2, tok

        def acc_view(m):
            return banks[m // 2].t[:, (m % 2) * T:(m % 2) * T + T]

        def accumulate(xh, xl, x_tok, first, last):
            wh, wl, wt = W.take()
            for m in range(KD):
                tok = mm3(acc_view(m), wh[:, c128(m)], wl[:, c128(m)], xh, xl, first and m % 2 == 0, last,
                          wt, x_tok, banks[m // 2].free if first else None, inc=(m == KD - 1))
            W.done(tok)
            return tok

        def add_accumulated(tok):
            for m in range(KD):
                x_tok[m] = tt(XT[:, m, :], XT[:, m, :], acc_view(m), ALU.add, tok, x_tok[m])
                banks[m // 2].free = x_tok[m]

        def norm_scale(bank, width, n, tok, dst, free=None):
            t = act(dst, bank.t[:, 0:width], ACT.Sqrt, tok, free, bias=EPSC[:, :], scale=1.0 / n)
            bank.free = t
            return recip(dst, dst, t)

        def rmsnorm(gain, sc, keep=None):
            SQ, TM, RS = sc.take3(KD, T), keep if keep is not None else sc.take3(KD, T), sc.take(T)
            bank = work()
            for m in range(KD):
                t = act(SQ[:, m, :], XT[:, m, :], ACT.Square, x_tok[m])
                tok = mm(bank.t[:, 0:T], ONES, SQ[:, m, :], m == 0, m == KD - 1, t, bank.free, inc=(m == KD - 1))
            rt = norm_scale(bank, T, D, tok, RS)
            pe = PE.last
            for m in range(KD):
                t = stt(TM[:, m, :], XT[:, m, :], par_col(gain, m), RS, ALU.mult, ALU.mult, rt, x_tok[m])
                t = split(TM[:, m, :], HH[:, m, :], HL[:, m, :], t, pe)
            return t

        t_x = S.dma(lambda e: e.dma_start(XT[:, :, :], xt), c_x)
        t_par = S.dma(lambda e: e.dma_start(PAR[:, :], par), c_par)
        t_con = S.dma(lambda e: e.dma_start(CON[:, :], con), c_con)
        for _ in range(NRAW):
            W.load()
        G.do(lambda e: e.memset(EPSC[:, :], EPS))
        t_one = G.do(lambda e: e.memset(ONEC[:, :], 1.0))
        for q in (PE, V, A):
            q.wait(t_par, t_con, t_one)
        x_tok = [t_x] * KD

        def late_const(name, dst, *toks):
            o, n = LCOL[name]
            return S.dma(lambda e: e.dma_start(dst, late[:, o:o + n]), c_late, *toks)

        sc = Scratch()
        INV = sc.take(1024)
        t_inv = late_const("invcnt", INV)
        H0 = sc.take3(KD, T)
        for _ in range(NSPLIT):
            W.split()
        rmsnorm("mix_norm0", sc, keep=H0)
        PA, PB = sc.take3(KD, T), sc.take3(KD, T)
        hl_tok = V.last
        toks = []
        for m in range(KD):
            g = m // 2
            w = 2
            src = H0[:, m, :]
            bufs = [PA[:, m, :], PB[:, m, :]]
            for step in range(g + 1):
                s = 1 << step
                dst = bufs[step % 2]
                vcopy(dst[:, 0:s], src[:, 0:s], V.last)
                tt(dst[:, s:T], src[:, s:T], src[:, 0:T - s], ALU.add, V.last)
                src = dst
            dst = bufs[(g + 1) % 2]
            tt(dst, src, INV[:, g * T:g * T + T], ALU.mult, V.last, t_inv)
            t = tt(dst, dst, H0[:, m, :], ALU.subtract, V.last)
            toks.append(split(dst, HH[:, m, :], HL[:, m, :], t, hl_tok))
        for half in range(2):
            wh, wl, wt = W.take()
            for g2 in range(2):
                g = 2 * half + g2
                for mo in range(2):
                    def wtile(k, base=512 * g2 + 128 * mo):
                        return wh[:, base + 256 * k:base + 256 * k + 128], wl[:, base + 256 * k:base + 256 * k + 128]
                    bank, tok = project_t(2, wtile, wt, HH[:, 2 * g:2 * g + 2, :], HL[:, 2 * g:2 * g + 2, :],
                                          toks[2 * g + 1])
                    m = 2 * g + mo
                    Y = PA[:, m, :]
                    bank.free = ts(Y, bank.t[:, 0:T], par_col("pool_b", m), par_col("pool_scale", m),
                                   ALU.add, ALU.mult, tok, V.last)
                    x_tok[m] = tt(XT[:, m, :], XT[:, m, :], Y, ALU.add, V.last)
            W.done(tok)

        def ffn(i):
            sync_all()
            sc = Scratch()
            h_tok = rmsnorm(f"ffn_norm{i}", sc)
            C, SI, GG = sc.take3(2, T), sc.take3(2, T), sc.take3(2, T)
            g_tok, acc_tok = [None] * JF, [None] * JF

            def out_block(j):
                acc_tok[j] = accumulate(GH[:, j % 2, :], GL[:, j % 2, :], g_tok[j], j == 0, j == JF - 1)

            for j in range(JF):
                s = j % 2
                gb, g_pe = project_block(HH, HL, h_tok)
                vb, v_pe = project_block(HH, HL, h_tok)
                if j:
                    out_block(j - 1)
                before = g_tok[j - 2] if j >= 2 else None
                cw = [par_col(f"conv{i}", 22 * t + j) for t in range(3)]
                a1 = act(C[:, s, :], gb.t[:, 0:T], ACT.Identity, g_pe, before,
                         bias=par_col(f"conv_b{i}", j), scale=cw[2])
                v1 = stt(C[:, s, 1:T], gb.t[:, 0:T - 1], cw[1], C[:, s, 1:T], ALU.mult, ALU.add, a1)
                v2 = stt(C[:, s, 2:T], gb.t[:, 0:T - 2], cw[0], C[:, s, 2:T], ALU.mult, ALU.add, v1)
                gb.free = v2
                a2 = act(SI[:, s, :], C[:, s, :], ACT.Silu, v2)
                v3 = tt(GG[:, s, :], SI[:, s, :], vb.t[:, 0:T], ALU.mult, a2, v_pe)
                vb.free = v3
                g_tok[j] = split(GG[:, s, :], GH[:, s, :], GL[:, s, :], v3, acc_tok[j - 2] if j >= 2 else PE.last)
            out_block(JF - 1)
            add_accumulated(acc_tok[JF - 1])

        def head_norm(bank, pe_tok, dst, gain, tmp, free=None):
            sq, rs = tmp
            t = vcopy(dst, bank.t[:, 0:T], pe_tok, free)
            bank.free = t
            t2 = act(sq, dst, ACT.Square, t, V.last, PE.last)
            nb = work()
            pt = mm(nb.t[:, 0:T], BLK64, sq, True, True, t2, nb.free, inc=True)
            rt = norm_scale(nb, T, 64, pt, rs, V.last)
            return stt(dst, dst, par_col(gain), rs, ALU.mult, ALU.mult, rt)

        def head_pair(m):
            return [(2 * m + a, slice(64 * a, 64 * a + 64)) for a in range(2)]

        def block_cols(kt, q0):
            return slice(q0, T) if kt == 0 else slice(q0 + 128, 384)

        def attention():
            sync_all()
            sc = Scratch()
            B = sc.take3(16, 384)
            t_b = S.dma(lambda e: e.dma_start(B, rev), c_rev)
            Q, K = sc.take3(KD, T), sc.take3(KD, T)
            VN = sc.take3(2, D)
            SS = sc.take3(16, 384)
            mark = sc.at
            h_tok = rmsnorm("mix_norm1", sc)
            tmps = [(sc.take(T), sc.take(T)) for _ in range(2)]
            for q_or_k, gain in ((Q, "attn_q_norm"), (K, "attn_k_norm")):
                for m in range(KD):
                    bank, tok = project_block(HH, HL, h_tok)
                    qk_tok = head_norm(bank, tok, q_or_k[:, m, :], gain, tmps[m % 2])
            for c, b2, tok in project_natural(HH, HL, h_tok, D):
                for t_ in range(2):
                    b2[t_].free = v_tok = act(VN[:, t_, 512 * c:512 * c + 512], b2[t_].t[:, :], ACT.Copy, tok)
            sc.at = mark
            PT = [sc.take(384), sc.take(384)]
            MX, NM, SM, RC = (sc.take(32) for _ in range(4))
            sync_all()
            V.wait(t_b)
            V.do(lambda e: e.memset(B[0:64, :, 64:128], -1e30))
            t_m = V.do(lambda e: e.memset(B[0:64, :, 320:384], -1e30))
            for h in range(16):
                m, rows = h // 2, slice(64 * (h % 2), 64 * (h % 2) + 64)
                bank = work()
                mm(bank.t[:, 0:128], Q[rows, m, 0:128], K[rows, m, 0:128], True, True, bank.free, qk_tok)
                tok = mm(bank.t[:, 128:384], Q[rows, m, 128:256], K[rows, m, :], True, True, inc=True)
                t = stt(SS[:, h, :], bank.t[:, 0:384], 0.125, B[:, h, :], ALU.mult, ALU.add, tok, t_m)
                bank.free = t
            for lo_, hi_, o in ((0, 128, 0), (128, 384, 16)):
                t = V.do(lambda e, lo_=lo_, hi_=hi_, o=o: e.tensor_reduce(MX[:, o:o + 16], SS[:, :, lo_:hi_], AX, ALU.max), t)
            t_nm = ts(NM, MX, -1.0, None, ALU.mult, None, t)
            e_tok = None
            for h in range(16):
                for lo_, hi_, o in ((0, 128, 0), (128, 384, 16)):
                    e_tok = act(SS[:, h, lo_:hi_], SS[:, h, lo_:hi_], ACT.Exp, t_nm,
                                bias=NM[:, o + h:o + h + 1], accum=SM[:, o + h:o + h + 1])
            t_rc = recip(RC, SM, e_tok)
            g_tok, acc_tok, pv_tok = [None] * KD, [None] * KD, [None] * 16
            for m in range(KD):
                ob = work()
                for h, rows in head_pair(m):
                    ts(SS[:, h, 0:128], SS[:, h, 0:128], RC[:, h:h + 1], None, ALU.mult, None, t_rc)
                    t = ts(SS[:, h, 128:384], SS[:, h, 128:384], RC[:, 16 + h:17 + h], None, ALU.mult, None, t_rc)
                    tb = work()
                    if tb is ob:
                        tb = work()
                    for i, src in enumerate((SS[:, h, 0:128], SS[:, h, 128:256], SS[:, h, 256:384])):
                        tok = PE.do(lambda e, o=tb.t[:, c128(i)], src=src: e.transpose(o, src, IDENT),
                                    t, tb.free, inc=(i == 2))
                    tb.free = t = act(PT[h % 2], tb.t[:, 0:384], ACT.Copy, tok, pv_tok[h - 2] if h >= 2 else None)
                    mm(ob.t[rows, 0:T], VN[:, 0, 64 * h:64 * h + 64], PT[h % 2][:, 0:T], True, False,
                       t, v_tok, ob.free)
                    pv_tok[h] = mm(ob.t[rows, 128:T], VN[:, 1, 64 * h:64 * h + 64], PT[h % 2][:, T:384],
                                   False, True, inc=True)
                s = m % 2
                free = acc_tok[m - 2] if m >= 2 else None
                th = act(GH[:, s, :], ob.t[:, 0:T], ACT.Copy, pv_tok[2 * m + 1], free)
                ob.free = g_tok[m] = tt(GL[:, s, :], ob.t[:, 0:T], GH[:, s, :].bitcast(F), ALU.subtract, th, free)
                if m:
                    acc_tok[m - 1] = accumulate(GH[:, 1 - s, :], GL[:, 1 - s, :], g_tok[m - 1], m == 1, False)
            add_accumulated(accumulate(GH[:, 1, :], GL[:, 1, :], g_tok[7], False, True))

        def mixers():
            sync_all()
            sc = Scratch()
            DEC = sc.take3(8, 384)
            NMASK = sc.take(384)
            CS, SN = sc.take(T), sc.take(T)
            for n, d in (("decay", DEC.rearrange("p a b -> p (a b)")), ("nmask", NMASK), ("cos", CS), ("sin", SN)):
                t_l = late_const(n, d)
            RQ, RK, SQ_, SK = (sc.take3(4, T) for _ in range(4))
            RV, SV = sc.take3(2, D), sc.take3(2, 512)
            RG, GA, GB = (sc.take3(KD, T) for _ in range(3))
            mark = sc.at
            h_tok = rmsnorm("norm_attn_2", sc)
            tmps = [(sc.take(T), sc.take(T)) for _ in range(2)]
            rope_tmp = [sc.take(T), sc.take(T)]

            def heads(dst, gain, rope):
                for m in range(4):
                    bank, tok = project_block(HH, HL, h_tok)
                    t = head_norm(bank, tok, dst[:, m, :], gain, tmps[m % 2])
                    if rope:
                        rb = work()
                        pt = mm(rb.t[:, 0:T], ROT, dst[:, m, :], True, True, t, rb.free, inc=True)
                        rt = rope_tmp[m % 2]
                        rb.free = tt(rt, rb.t[:, 0:T], SN, ALU.mult, pt, V.last, t_l)
                        tt(dst[:, m, :], dst[:, m, :], CS, ALU.mult, rb.free)
                        tt(dst[:, m, :], dst[:, m, :], rt, ALU.add, V.last)

            def natural(dst, n):
                for c, b2, tok in project_natural(HH, HL, h_tok, n):
                    for t_ in range(2):
                        b2[t_].free = act(dst[:, t_, 512 * c:512 * c + 512], b2[t_].t[:, :], ACT.Copy, tok)

            def gates(dst, f):
                for m in range(KD):
                    bank, tok = project_block(HH, HL, h_tok)
                    bank.free = act(dst[:, m, :], bank.t[:, 0:T], f, tok)

            heads(RQ, "ret_q_norm", True)
            heads(RK, "ret_k_norm", True)
            natural(RV, D)
            gates(RG, ACT.Silu)
            heads(SQ_, "sb_q_norm", False)
            heads(SK, "sb_k_norm", False)
            natural(SV, 512)
            gates(GA, ACT.Sigmoid)
            gates(GB, ACT.Sigmoid)
            sync_all()
            sc.at = mark

            Z, L, NS_ = (sc.take3(8, 384) for _ in range(3))
            z_tok = []
            for h in range(8):
                m, rows = h // 2, slice(64 * (h % 2), 64 * (h % 2) + 64)
                bank = work()
                mm(bank.t[:, 0:T], SK[rows, m, 0:128], SQ_[rows, m, :], True, True, bank.free)
                tok = mm(bank.t[:, T:384], SK[rows, m, 128:T], SQ_[rows, m, 128:T], True, True, inc=True)
                t = act(Z[:, h, :], bank.t[:, 0:384], ACT.Copy, tok, scale=0.125)
                bank.free = t
                z_tok.append(act(L[:, h, :], Z[:, h, :], ACT.Abs, t))
            e_tok = [act(L[:, h, :], L[:, h, :], ACT.Exp, z_tok[h], scale=-1.0) for h in range(8)]
            l_tok = [act(L[:, h, :], L[:, h, :], ACT.Ln, e_tok[h], bias=ONEC[:, :]) for h in range(8)]
            w_tok = []
            for h in range(8):
                t = stt(NS_[:, h, :], Z[:, h, :], 0.0, L[:, h, :], ALU.max, ALU.add, l_tok[h])
                t = tt(NS_[:, h, :], NS_[:, h, :], NMASK, ALU.mult, t)
                t2 = stt(Z[:, h, :], Z[:, h, :], 0.0, L[:, h, :], ALU.min, ALU.subtract, t)
                bank = work()
                mm(bank.t[:, 0:T], TRI, NS_[:, h, 0:T], True, False, bank.free, t)
                mm(bank.t[:, 128:T], ONES, NS_[:, h, T:384], False, False)
                tok = mm(bank.t[:, T:384], TRI, NS_[:, h, T:384], False, True, inc=True)
                t = tt(Z[:, h, :], Z[:, h, :], bank.t[:, 0:384], ALU.add, tok, t2)
                bank.free = t
                w_tok.append(act(L[:, h, :], Z[:, h, :], ACT.Exp, t))
            h_free = PE.last
            for m in range(4):
                ob = work()
                for h, rows in head_pair(m):
                    t = stt(L[:, h, :], L[:, h, :], -1.0, NMASK, ALU.mult, ALU.mult, w_tok[h])
                    mm(ob.t[rows, 0:T], SV[:, 0, 64 * h:64 * h + 64], L[:, h, 0:T], True, False, t, ob.free)
                    tok = mm(ob.t[rows, 128:T], SV[:, 1, 64 * h:64 * h + 64], L[:, h, T:384], False, True, inc=True)
                th = act(HH[:, m, :], ob.t[:, 0:T], ACT.Copy, tok, h_free)
                ob.free = t = tt(HL[:, m, :], ob.t[:, 0:T], HH[:, m, :].bitcast(F), ALU.subtract, th, h_free)
            for b in range(4):
                wh, wl, wt = W.take()
                for g in range(2):
                    m = 2 * b + g

                    def wtile(k, base=512 * g):
                        return wh[:, base + 128 * k:base + 128 * k + 128], wl[:, base + 128 * k:base + 128 * k + 128]

                    bank, tok = project_t(4, wtile, wt, HH, HL, t)
                    bank.free = tt(GB[:, m, :], GB[:, m, :], bank.t[:, 0:T], ALU.mult, tok)
                W.done(tok)

            sync_all()
            sc.at = mark
            ST = [sc.take(384), sc.take(384)]
            YB = [sc.take(T), sc.take(T)]
            YQ = [sc.take(T), sc.take(T)]
            RS = [sc.take(T), sc.take(T)]
            y_free = [None, None]
            s_free = [None, None]
            for h in range(8):
                m, rows, s = h // 2, slice(64 * (h % 2), 64 * (h % 2) + 64), h % 2
                bank = work()
                mm(bank.t[:, 0:T], RK[rows, m, 0:128], RQ[rows, m, :], True, True, bank.free)
                tok = mm(bank.t[:, T:384], RK[rows, m, 128:T], RQ[rows, m, 128:T], True, True, inc=True)
                bank.free = t = tt(ST[s], bank.t[:, 0:384], DEC[:, h, :], ALU.mult, tok, s_free[s])
                yb = work()
                mm(yb.t[:, 0:T], RV[:, 0, c128(h)], ST[s][:, 0:T], True, False, t, yb.free)
                tok = mm(yb.t[:, 128:T], RV[:, 1, c128(h)], ST[s][:, T:384], False, True, inc=True)
                s_free[s] = tok
                t = vcopy(YB[s], yb.t[:, 0:T], tok, y_free[s])
                yb.free = t
                mb = work()
                tok = mm(mb.t[:, 0:T], ONES, YB[s], True, True, t, mb.free, inc=True)
                t = stt(YB[s], mb.t[:, 0:T], -1.0 / 128, YB[s], ALU.mult, ALU.add, tok)
                mb.free = t
                t2 = act(YQ[s], YB[s], ACT.Square, t, y_free[s])
                qb = work()
                tok = mm(qb.t[:, 0:T], ONES, YQ[s], True, True, t2, qb.free, inc=True)
                t = norm_scale(qb, T, 128, tok, RS[s], y_free[s])
                t = stt(YB[s], YB[s], par_col("group_norm", h), RS[s], ALU.mult, ALU.mult, t)
                t = tt(YB[s], YB[s], RG[:, h, :], ALU.mult, t)
                y_free[s] = t = split(YB[s], HH[:, h, :], HL[:, h, :], t)
            g_tok, acc_tok = [None] * KD, [None] * KD
            MX_ = [sc.take(T), sc.take(T)]
            h_tok = t
            for m in range(KD):
                s = m % 2
                bank, tok = project_block(HH, HL, h_tok)
                bank.free = t = tt(MX_[s], GA[:, m, :], bank.t[:, 0:T], ALU.mult, tok, g_tok[m - 2] if m >= 2 else None)
                t = tt(MX_[s], MX_[s], GB[:, m, :], ALU.add, t)
                g_tok[m] = split(MX_[s], GH[:, s, :], GL[:, s, :], t, acc_tok[m - 2] if m >= 2 else None)
                if m:
                    acc_tok[m - 1] = accumulate(GH[:, 1 - s, :], GL[:, 1 - s, :], g_tok[m - 1], m == 1, False)
            add_accumulated(accumulate(GH[:, 1, :], GL[:, 1, :], g_tok[7], False, True))

        def peer():
            sync_all()
            sc = Scratch()
            BIG3 = BIG[:, :].rearrange("p (c t) -> p c t", t=T)
            KEY = sc.take3(2, 128)
            t_key = S.dma(lambda e: e.dma_start(KEY, keys), c_key)
            QT = sc.take3(16, T)
            I1F, I2F, GT = (sc.take3(8, 16) for _ in range(3))
            mark = sc.at
            h_tok = rmsnorm("norm_ffn_2", sc)
            for l in range(16):
                bank, tok = project_block(HH, HL, h_tok)
                bank.free = q_tok = act(QT[:, l, :], bank.t[:, 0:T], ACT.Copy, tok)
            sync_all()
            sc.at = mark
            SC_ = [sc.take3(16, 128), sc.take3(16, 128)]
            S2 = sc.take(256)
            TV = sc.take3(16, 16)
            TI = sc.take3(16, 16).bitcast(U32)
            CV = sc.take3(8, 16)
            CI = sc.take3(8, 16).bitcast(U32)
            AB = sc.take3(8, 16).bitcast(U32)
            AF = sc.take3(8, 16)
            IF = sc.take3(16, 16)
            CAND = sc.take(2048)
            OH = sc.take(2048)
            SMX = sc.take(8)
            SC4 = CAND.rearrange("p (h a b) -> p h a b", h=8, a=16)
            OH4 = OH.rearrange("p (h a b) -> p h a b", h=8, a=16)

            def scores(tt_):
                for q4 in range(4):
                    bank = work()
                    for l in range(4 * q4, 4 * q4 + 4):
                        tok = mm(bank.t[:, c128(l % 4)], QT[:, l, c128(tt_)], KEY[:, l % 2, :], True, True,
                                 q_tok, t_key, bank.free, inc=(l % 4 == 3))
                    bank.free = t = act(SC_[tt_][:, 4 * q4:4 * q4 + 4, :], bank.t[:, :].rearrange("p (a b) -> p a b", b=128),
                                        ACT.Copy, tok)
                return t

            def top16(src, work_, vals, idx, tok):
                V.do(lambda e: e.max(vals[:, 0:8], src), tok, V.last)
                V.do(lambda e: e.max_index(idx[:, 0:8], vals[:, 0:8], src), V.last)
                V.do(lambda e: e.match_replace(work_, vals[:, 0:8], src, NEG), V.last)
                V.do(lambda e: e.max(vals[:, 8:16], work_), V.last)
                return V.do(lambda e: e.max_index(idx[:, 8:16], vals[:, 8:16], work_), V.last)

            def bc(ap, axis):
                return ap.unsqueeze(axis).to_broadcast([128, 8, 16, 16])

            def route(tt_, tok):
                ops = []
                for l in range(16):
                    ops.append(lambda l=l: top16(SC_[tt_][:, l, :], S2[:, 0:128], TV[:, l, :], TI[:, l, :], tok))

                def cand():
                    TVh = TV.rearrange("p (h s) k -> p h s k", s=2)
                    tt(SC4, bc(TVh[:, :, 0, :], 3), bc(TVh[:, :, 1, :], 2), ALU.add, V.last)
                ops.append(cand)
                for h in range(8):
                    ops.append(lambda h=h: top16(CAND[:, 256 * h:256 * h + 256], S2, CV[:, h, :], CI[:, h, :], V.last))

                def pick():
                    vcopy(IF, TI, V.last)
                    IFh = IF.rearrange("p (h s) k -> p h s k", s=2)
                    for side, dst in ((0, I1F), (1, I2F)):
                        if side == 0:
                            V.do(lambda e: e.tensor_scalar(AB, CI, 4, None, ALU.logical_shift_right), V.last)
                        else:
                            V.do(lambda e: e.tensor_scalar(AB, CI, 15, None, ALU.bitwise_and), V.last)
                        vcopy(AF, AB, V.last)
                        i16 = IOTA[:, 0:16].unsqueeze(1).unsqueeze(1).to_broadcast([128, 8, 16, 16])
                        tt(OH4, bc(AF, 3), i16, ALU.is_equal, V.last)
                        tt(OH4, OH4, bc(IFh[:, :, side, :], 2), ALU.mult, V.last)
                        V.do(lambda e, dst=dst: e.tensor_reduce(dst, OH4, AX, ALU.add), V.last)
                    t = tt(GT, CV, CV[:, :, 0:1].to_broadcast([128, 8, 16]), ALU.subtract, V.last)
                    t = act(GT, GT, ACT.Exp, t)
                    V.do(lambda e: e.tensor_reduce(SMX, GT, AX, ALU.add), t)
                    recip(SMX, SMX, V.last)
                    t = tt(GT, GT, SMX.unsqueeze(2).to_broadcast([128, 8, 16]), ALU.mult, V.last)
                    bank = work()
                    for i, src in enumerate((I1F, I2F, GT)):
                        flat = src.rearrange("p a b -> p (a b)")
                        tok2 = PE.do(lambda e, i=i, flat=flat: e.transpose(bank.t[:, c128(i)], flat, IDENT),
                                     t, bank.free, inc=(i == 2))
                    bank.free = vcopy(RT[:, :, c128(tt_)], bank.t[:, 0:384].rearrange("p (a b) -> p a b", b=128), tok2)
                ops.append(pick)
                return ops

            s_tok = [scores(0), scores(1)]
            todo = route(0, s_tok[0]) + route(1, s_tok[1])

            lowest = sc.at // T
            a_tok = [None] * 128
            for c in range(128):
                if c == lowest:
                    while todo:
                        todo.pop(0)()
                    sync_all()
                bank, tok = project_block(HH, HL, h_tok)
                a_tok[c] = bank.free = act(BIG3[:, c, :], bank.t[:, 0:T], ACT.Gelu_apprx_tanh, tok)
                if todo:
                    todo.pop(0)()
            sync_all()
            vcopy(GS[:, 0, :], RT[:, 2, :], V.last)
            tg = tt(GS[:, 1, :], RT[:, 2, :], GS[:, 0, :].bitcast(F), ALU.subtract, V.last)
            HHf = HH[:, :, :].rearrange("p k t -> p (k t)")
            HLf = HL[:, :, :].rearrange("p k t -> p (k t)")
            o_free = [PE.last, PE.last]
            t_a = V.last
            for q in range(T // 4):
                s = q % 2
                bank = work()
                for i in range(4):
                    t = 4 * q + i
                    o1 = HHf[:, 1024 * s + 128 * i:1024 * s + 128 * i + 128]
                    oh = HHf[:, 1024 * s + 512 + 128 * i:1024 * s + 640 + 128 * i]
                    ol = HLf[:, 1024 * s + 128 * i:1024 * s + 128 * i + 128]
                    ts(o1, IOTA, RT[:, 0, t:t + 1], None, ALU.is_equal, None, o_free[s], tg)
                    ts(oh, IOTA, RT[:, 1, t:t + 1], GS[:, 0, t:t + 1].bitcast(F), ALU.is_equal, ALU.mult)
                    tv = ts(ol, IOTA, RT[:, 1, t:t + 1], GS[:, 1, t:t + 1].bitcast(F), ALU.is_equal, ALU.mult)
                    mm(bank.t[:, c128(i)], o1, oh, i == 0, False, tv, bank.free)
                    tok = mm(bank.t[:, c128(i)], o1, ol, False, i == 3, inc=(i == 3))
                o_free[s] = tok
                dst = BIG3[:, :, 4 * q:4 * q + 4]
                bank.free = t_a = tt(dst, dst, bank.t[:, :].rearrange("p (t c) -> p c t", t=4), ALU.mult, tok)
            a_split = [None] * 128
            acc_tok = [None] * 128
            for c in range(128):
                s = c % 2
                a_split[c] = split(BIG3[:, c, :], GH[:, s, :], GL[:, s, :], t_a, acc_tok[c - 2] if c >= 2 else PE.last)
                if c:
                    acc_tok[c - 1] = accumulate(GH[:, 1 - s, :], GL[:, 1 - s, :], a_split[c - 1], c == 1, False)
            add_accumulated(accumulate(GH[:, 1, :], GL[:, 1, :], a_split[127], False, True))

        if upto >= 1:
            ffn(0)
        if upto >= 2:
            attention()
        if upto >= 3:
            ffn(1)
        if upto >= 4:
            mixers()
        if upto >= 5:
            peer()
        for c in c_raw:
            if c[1]:
                S.wait((c[0], c[1]))
        S.wait(*x_tok)
        t_o = S.dma(lambda e: e.dma_start(out, XT[:, :, :]), c_out)
        S.wait(t_o)

        block = ctx.enter_context(nc.Block())

        @block.sync
        def _(e):
            S.replay(e)

        @block.scalar
        def _(e):
            A.replay(e)

        @block.vector
        def _(e):
            V.replay(e)

        @block.gpsimd
        def _(e):
            G.replay(e)

        @block.tensor
        def _(e):
            PE.replay(e)


def _vec(v):
    return v.reshape(-1, 128).T


def _cols(w):
    k, n = w.shape
    return w.reshape(k // 128, 128, n // 128, 128).transpose(2, 1, 0, 3).reshape(n // 128, 128, k)


def _natural(w):
    k, n = w.shape
    return w.reshape(4, 2, 128, n // 512, 512).transpose(3, 0, 2, 1, 4).reshape(-1, 128, BLK)


def _wall(i):
    w = np.empty((N_BLOCKS, 128, BLK), np.float32)
    at = 0

    def put(b):
        nonlocal at
        w[at:at + len(b)] = b
        at += len(b)

    def ffn(l):
        nonlocal at
        g, v, o = _cols(i["ffn_w_gate"][l]), _cols(i["ffn_w_val"][l]), i["ffn_w_out"][l].reshape(JF, 128, D)
        for j in range(JF):
            w[at], w[at + 1] = g[j], v[j]
            at += 2
            if j:
                w[at] = o[j - 1]
                at += 1
        w[at] = o[JF - 1]
        at += 1

    put(i["pool_w"][0].reshape(2, 2, 2, 128, 256).transpose(0, 3, 1, 2, 4).reshape(2, 128, BLK))
    ffn(0)
    put(_cols(i["attn_wqkv"][0][:, 0:2048]))
    put(_natural(i["attn_wqkv"][0][:, 2048:3072]))
    put(i["attn_wo"][0].reshape(8, 128, D))
    ffn(1)
    wi = i["w_in_2"][0]
    put(_cols(wi[:, 0:1024]))
    put(_natural(wi[:, 1024:2048]))
    put(_cols(wi[:, 2048:4096]))
    put(_natural(wi[:, 4096:4608]))
    put(_cols(wi[:, 4608:6656]))
    put(_cols(i["w_branch_sb_2"][0]).reshape(4, 2, 128, 512).transpose(0, 2, 1, 3).reshape(4, 128, BLK))
    br, wo = _cols(i["w_branch_ret_2"][0]), i["w_out_2"][0].reshape(8, 128, D)
    for m in range(8):
        w[at] = br[m]
        at += 1
        if m:
            w[at] = wo[m - 1]
            at += 1
    w[at] = wo[7]
    at += 1
    put(_cols(i["peer_w_q_2"][0]))
    u = i["peer_u_2"][0].reshape(128, 128, 8, 128)
    put(u.transpose(1, 3, 2, 0).reshape(128, 128, BLK))
    put(i["peer_v_2"][0].reshape(128, 128, D).transpose(1, 0, 2))
    assert at == N_BLOCKS
    return w


def _params(i):
    def two(v):
        return np.concatenate([v, v]).reshape(128, 1)

    cols = [_vec(i["mix_norm"][0]), _vec(i["mix_norm"][1]), _vec(i["ffn_norm"][0]), _vec(i["ffn_norm"][1]),
            _vec(i["pool_b"][0]), _vec(i["pool_scale"][0]), two(i["attn_q_norm"][0]), two(i["attn_k_norm"][0])]
    cols += [_vec(i["ffn_conv_w"][l].reshape(-1)) for l in range(2)]
    cols += [_vec(i["ffn_conv_b"][l]) for l in range(2)]
    cols += [_vec(i["norm_attn_2"][0]), two(i["ret_q_norm_2"][0]), two(i["ret_k_norm_2"][0]),
             _vec(i["ret_group_norm_2"][0]), two(i["sb_q_norm_2"][0]), two(i["sb_k_norm_2"][0]),
             _vec(i["norm_ffn_2"][0])]
    return np.ascontiguousarray(np.concatenate(cols, axis=1))


def _relative(table):
    q = np.arange(128)[:, None]
    at = np.concatenate([256 + q - np.arange(128)[None, :], 384 + q - np.arange(T)[None, :]], axis=1)
    return np.ascontiguousarray(table[:, at].transpose(1, 0, 2))


def _constants():
    c = np.zeros((128, NCON), np.float32)
    p = np.arange(128)
    c[:, 0:128] = np.eye(128)
    c[:, 128:256] = 1.0
    c[:, 256:384] = p[:, None] // 64 == p[None, :] // 64
    same = p[:, None] // 64 == p[None, :] // 64
    k, m = p[:, None] % 64, p[None, :] % 64
    c[:, 384:512] = same * (1.0 * (k == m - 32) - 1.0 * (k == m + 32))
    c[:, 512:640] = p[:, None] > p[None, :]
    c[:, 640:768] = p[None, :]
    late = np.zeros((128, NLATE), np.float32)
    t = np.arange(T)
    for g, w in enumerate((2, 4, 8, 16)):
        late[:, g * T:g * T + T] = (1.0 / np.minimum(t + 1, w))[None, :]
    keys = p[:, None]
    qpos = np.concatenate([t, t[128:]])[None, :]
    kpos = keys + np.concatenate([np.zeros(T), np.full(128, 128)])[None, :]
    diff = qpos - kpos
    for h in range(8):
        lg = np.log1p(-np.exp2(-5.0 - h))
        late[:, 1024 + 384 * h:1408 + 384 * h] = np.where(diff >= 0, np.exp(lg * np.maximum(diff, 0)), 0.0) * 0.125
    freqs = (10000.0 ** (-np.arange(32, dtype=np.float32) / 32)).astype(np.float32)
    ang = (t[None, :].astype(np.float32) * freqs[p % 32][:, None]).astype(np.float32).astype(np.float64)
    late[:, 4096:4352] = np.cos(ang)
    late[:, 4352:4608] = np.sin(ang)
    late[:, 4608:4992] = -1.0 * (diff > 0)
    return c, late


def kernel(**inputs):
    import concourse.bacc as bacc
    from concourse.bass_utils import run_bass_kernel_spmd

    i = {n: np.asarray(a) for n, a in inputs.items()}
    con, late = _constants()
    arrays = {
        "wall": _wall(i),
        "par": _params(i),
        "con": con,
        "late": late,
        "xt": np.ascontiguousarray(i["x"][0].reshape(T, KD, 128).transpose(2, 1, 0)),
        "rev": _relative(i["attn_rel_bias"][0]),
        "keys": np.ascontiguousarray(np.stack([i["peer_sub_keys_1_2"][0].T, i["peer_sub_keys_2_2"][0].T], axis=1)),
    }
    nc = bacc.Bacc("TRN2", target_bir_lowering=False, num_devices=1)
    args = [nc.dram_tensor(n, a.shape, F, kind="ExternalInput").ap() for n, a in arrays.items()]
    out = nc.dram_tensor("out", (128, KD, T), F, kind="ExternalOutput").ap()
    build(nc, *args, out)
    r = run_bass_kernel_spmd(nc, [arrays], core_ids=[0])
    got = r.results[0]["out"]
    return np.ascontiguousarray(got.transpose(2, 1, 0)).reshape(1, T, D)
```

```python
import math
from contextlib import ExitStack

import numpy as np

import concourse.bass as bass
from concourse import mybir

F = mybir.dt.float32
R = mybir.dt.float32r
U32 = mybir.dt.uint32
B16 = mybir.dt.bfloat16
ALU = mybir.AluOpType
ACT = mybir.ActivationFunctionType
AX = mybir.AxisListType.X

T = 256
D = 1024
KD = D // 128
FF = 2816
JF = FF // 128
EPS = 1e-6
NRAW = 4
NSPLIT = 3
BLK = 1024
N_POOL, N_FFN, N_ATT = 2, 3 * JF, 32
N_IN, N_BR, N_PQ = 52, 20, 16
N_BLOCKS = N_POOL + 2 * N_FFN + N_ATT + N_IN + N_BR + N_PQ + 256
NEG = -3.4028234663852886e38
RATE_A, RATE_M, RATE_R, RATE_G = 1.0, 1.0, 1.0, 1.0
POOL_PEER = 4

_PARAMS = [("mix_norm0", 8), ("mix_norm1", 8), ("ffn_norm0", 8), ("ffn_norm1", 8), ("pool_b", 8),
           ("pool_scale", 8), ("attn_q_norm", 1), ("attn_k_norm", 1), ("conv0", 66), ("conv1", 66),
           ("conv_b0", 22), ("conv_b1", 22), ("norm_attn_2", 8), ("ret_q_norm", 1), ("ret_k_norm", 1),
           ("group_norm", 8), ("sb_q_norm", 1), ("sb_k_norm", 1), ("norm_ffn_2", 8)]
PCOL = {}
NPAR = 0
for _n, _w in _PARAMS:
    PCOL[_n] = NPAR
    NPAR += _w

CCOL = {}
NCON = 0
for _n, _w in [("ident", 128), ("one", 1), ("blk2", 2), ("sel2", 512), ("rot", 128), ("tri", 128), ("ones", 128),
               ("cen", 128), ("sel1", 512), ("decay", 3072), ("nmask", 384), ("cos", 256), ("sin", 256),
               ("invcnt", 64), ("iota", 128)]:
    CCOL[_n] = (NCON, _w)
    NCON += _w
NCOMMON = 129


class Queue:

    def __init__(self, sem):
        self.sem, self.count, self.items, self.seen = sem, 0, [], {}

    def wait(self, *toks):
        for t in toks:
            if t is None:
                continue
            if isinstance(t, list):
                self.wait(*t)
                continue
            sem, val = t
            if val and self.seen.get(sem.name, 0) < val:
                self.seen[sem.name] = val
                self.items.append(("w", sem, val))

    def do(self, fn, *toks, inc=True):
        self.wait(*toks)
        if inc:
            self.count += 1
        self.items.append(("i", fn, (self.sem, 1) if inc else None))
        return (self.sem, self.count)

    def dma(self, fn, chan, *toks):
        self.wait(*toks)
        chan[1] += 16
        self.items.append(("i", fn, (chan[0], 16)))
        return (chan[0], chan[1])

    @property
    def last(self):
        return (self.sem, self.count)

    def replay(self, eng):
        for kind, a, b in self.items:
            if kind == "w":
                eng.wait_ge(a, b)
            else:
                ins = a(eng)
                if b:
                    ins.then_inc(*b)


class Bank:
    def __init__(self, t):
        self.t, self.free = t, None


class Pool:

    def __init__(self, banks):
        self.banks = list(banks)

    def has(self, n=1):
        return len(self.banks) >= n

    def get(self):
        return self.banks.pop(0)

    def put(self, bank, tok):
        bank.free = tok
        self.banks.append(bank)


class Tasks:

    def __init__(self):
        self.live, self.credit, self.rate = [], 0.0, 1.0

    def add(self, gen):
        self.live.append(gen)

    def step(self):
        for g in list(self.live):
            try:
                next(g)
            except StopIteration:
                self.live.remove(g)

    def tick(self):
        self.credit += self.rate
        while self.credit >= 1.0:
            self.credit -= 1.0
            self.step()

    def drain(self):
        while self.live:
            self.step()


def build(nc, wall, par, con, xt, rel, keys, out, upto=99):
    ctx = ExitStack()
    with ctx:
        def sb(name, shape, dt=F, where=None):
            return (where or ctx).enter_context(nc.sbuf_tensor(name, shape, dt))

        def sem(name):
            return ctx.enter_context(nc.semaphore(name))

        XT = sb("XT", [128, KD, T])
        HH = sb("HH", [128, KD, T], R)
        HL = sb("HL", [128, KD, T], R)
        GH = sb("GH", [128, 2, T], R)
        GL = sb("GL", [128, 2, T], R)
        RAW = sb("RAW", [128, NRAW, BLK])
        WH = sb("WH", [128, NSPLIT, BLK], R)
        WL = sb("WL", [128, NSPLIT, BLK], R)
        PAR = sb("PAR", [128, NPAR])
        COM = sb("COM", [128, NCOMMON])
        EPSC = sb("EPSC", [128, 1])
        ONEC = sb("ONEC", [128, 1])
        banks = [Bank(ctx.enter_context(nc.psum_tensor(f"ps{i}", [128, 512], F))) for i in range(8)]

        PE, V, A, G, S = (Queue(sem(n)) for n in ("s_pe", "s_dve", "s_act", "s_pool", "s_sp"))
        c_par, c_con, c_late, c_x, c_rel, c_key, c_out = ([sem(n), 0] for n in (
            "d_par", "d_con", "d_late", "d_x", "d_rel", "d_key", "d_out"))
        c_raw = [[sem(f"d_raw{i}"), 0] for i in range(NRAW)]
        IDENT, ONE = COM[:, 0:128], COM[:, 128:129]

        def par_col(name, j=0):
            c = PCOL[name] + j
            return PAR[:, c:c + 1]

        def mm(o, l, r, start, stop, *toks, inc=False):
            return PE.do(lambda e: e.matmul(o, l, r, start=start, stop=stop, skip_group_check=True), *toks, inc=inc)

        def transpose(o, i, *toks, inc=False):
            return PE.do(lambda e: e.transpose(o, i, IDENT), *toks, inc=inc)

        def act(o, i, f, *toks, bias=None, scale=None, accum=None):
            kw = {}
            if bias is not None:
                kw["bias"] = bias
            if scale is not None:
                kw["scale"] = scale
            if accum is not None:
                kw["accum_out"] = accum
            return A.do(lambda e: e.activation(o, i, f, **kw), *toks)

        def tt(o, a, b, op, *toks, q=None):
            return (q or V).do(lambda e: e.tensor_tensor(o, a, b, op), *toks)

        def ts(o, a, s1, s2, op0, op1, *toks):
            if op1 is None:
                return V.do(lambda e: e.tensor_scalar(o, a, s1, None, op0), *toks)
            return V.do(lambda e: e.tensor_scalar(o, a, s1, s2, op0, op1), *toks)

        def stt(o, a, s, b, op0, op1, *toks):
            return V.do(lambda e: e.scalar_tensor_tensor(out=o, in0=a, scalar=s, in1=b, op0=op0, op1=op1), *toks)

        def vcopy(o, a, *toks):
            return V.do(lambda e: e.tensor_copy(o, a), *toks)

        def reduce_(o, i, op, *toks):
            return V.do(lambda e: e.tensor_reduce(o, i, AX, op), *toks)

        def split(src, hi, lo, ready, *frees, q=None):
            th = act(hi, src, ACT.Copy, ready, *frees)
            return tt(lo, src, hi.bitcast(F), ALU.subtract, th, ready, *frees, q=q)

        def sync_all():
            lasts = [q.last for q in (PE, V, A, G)]
            for q in (PE, V, A, G, S):
                q.wait(*lasts)

        class Weights:
            def __init__(self):
                self.loaded = self.splitted = 0
                self.order = []
                self.pending = 0
                self.on_pool = 0
                self.raw_free = [None] * NRAW
                self.free = [None] * NSPLIT
                self.raw_tok, self.tok = {}, {}

            def load(self):
                b = self.loaded
                if b >= N_BLOCKS:
                    return
                s = b % NRAW
                self.raw_tok[b] = S.dma(lambda e: e.dma_start(RAW[:, s, :], wall[b]), c_raw[s], self.raw_free[s])
                self.loaded += 1

            def split(self):
                b = self.splitted
                if b >= N_BLOCKS:
                    return
                r, s = b % NRAW, b % NSPLIT
                q = G if self.on_pool and b % self.on_pool == 0 else V
                self.tok[b] = split(RAW[:, r, :], WH[:, s, :], WL[:, s, :], self.raw_tok[b], self.free[s], q=q)
                self.raw_free[r] = self.tok[b]
                self.splitted += 1
                self.load()

            def take(self, *name):
                b = len(self.order)
                if b not in self.tok:
                    self.pump()
                self.order.append(name)
                s = b % NSPLIT
                return WH[:, s, :], WL[:, s, :], self.tok[b]

            def done(self, tok):
                self.pump()
                self.free[(len(self.order) - 1) % NSPLIT] = tok
                self.pending = 1

            def pump(self):
                if self.pending:
                    self.pending = 0
                    self.split()

        W = Weights()
        tasks = Tasks()

        def half_way():
            W.pump()
            tasks.tick()

        def mm3(o, lh, ll, rh, rl, first, last, *toks, inc=False):
            mm(o, lh, rh, first, False, *toks)
            mm(o, lh, rl, False, False)
            return mm(o, ll, rh, False, last, inc=inc)

        def c128(i):
            return slice(128 * i, 128 * i + 128)

        def project_t(pool, nk, wtile, lhs_tok, hi, lo, h_tok):
            bank = pool.get()
            for k in range(nk):
                wh, wl = wtile(k)
                tok = mm3(bank.t[:, 0:T], wh, wl, hi[:, k, :], lo[:, k, :], k == 0, k == nk - 1,
                          lhs_tok, h_tok[k], bank.free, inc=(k == nk - 1))
                if k == 3 and nk == KD:
                    half_way()
            return bank, tok

        def project_block(pool, name, idx, hi, lo, h_tok):
            wh, wl, wt = W.take(name, idx)
            bank, tok = project_t(pool, KD, lambda k: (wh[:, c128(k)], wl[:, c128(k)]), wt, hi, lo, h_tok)
            W.done(tok)
            return bank, tok

        def project_natural(pool, name, dst, ncols, h_tok, parts=None):
            for c in range(ncols // 512):
                b2 = [pool.get(), pool.get()]
                for kb in range(4):
                    wh, wl, wt = W.take(name, 4 * c + kb)
                    for t_ in range(2):
                        for k2 in range(2):
                            k = 2 * kb + k2
                            tok = mm3(b2[t_].t[:, :], HH[:, k, c128(t_)], HL[:, k, c128(t_)],
                                      wh[:, 512 * k2:512 * k2 + 512], wl[:, 512 * k2:512 * k2 + 512],
                                      k == 0, k == KD - 1, wt, h_tok[k], b2[t_].free, inc=True)
                        if t_ == 0:
                            half_way()
                    W.done(tok)
                    tasks.tick()
                for t_ in range(2):
                    last = act(dst[:, t_, 512 * c:512 * c + 512], b2[t_].t[:, :], ACT.Copy, tok)
                    pool.put(b2[t_], last)
                if parts is not None:
                    parts[c] = last
            return last

        def acc_view(m):
            return banks[m // 2].t[:, (m % 2) * T:(m % 2) * T + T]

        def accumulate(name, idx, xh, xl, x_tok, first, last):
            wh, wl, wt = W.take(name, idx)
            for m in range(KD):
                tok = mm3(acc_view(m), wh[:, c128(m)], wl[:, c128(m)], xh, xl, first and m % 2 == 0, last,
                          wt, x_tok, banks[m // 2].free if first else None, inc=(m == KD - 1))
                if m == 3:
                    half_way()
            W.done(tok)
            return tok

        def add_accumulated(tok):
            for m in range(KD):
                x_tok[m] = tt(XT[:, m, :], XT[:, m, :], acc_view(m), ALU.add, tok, x_tok[m])
                banks[m // 2].free = x_tok[m]

        def inverse_root(sums, n, tmp, tok):
            r, ms, y = tmp
            ta = act(r, sums, ACT.Sqrt, tok, V.last, bias=EPSC[:, :], scale=1.0 / n)
            free = ts(ms, sums, 1.0 / n, EPS, ALU.mult, ALU.add, ta)
            V.do(lambda e: e.reciprocal(r, r), ta)
            tt(y, r, r, ALU.mult, V.last)
            tt(y, y, ms, ALU.mult, V.last)
            ts(y, y, -0.5, 1.5, ALU.mult, ALU.add, V.last)
            return tt(r, r, y, ALU.mult, V.last), free

        def rmsnorm(gain, SQ, TM, sm, b1, b2, write):
            nsq, ntm = SQ.shape[1], TM.shape[1]
            sq_free, tm_free = [None] * nsq, [None] * ntm
            for m in range(KD):
                s = m % nsq
                t = act(SQ[:, s, :], XT[:, m, :], ACT.Square, x_tok[m], sq_free[s])
                for i in range(2):
                    tok = mm(b1.t[:, i:i + 1], SQ[:, s, c128(i)], ONE, m == 0 and i == 0, m == KD - 1, t, b1.free,
                             inc=(i == 1))
                sq_free[s] = tok
            tr, b1.free = inverse_root(b1.t[:, 0:2], D, [x[:, 0:2] for x in sm], tok)
            for i in range(2):
                tok = mm(b2.t[:, c128(i)], sm[0][:, i:i + 1].to_broadcast([128, 128]), IDENT, True, True,
                         tr, b2.free, inc=(i == 1))
            toks = []
            for m in range(KD):
                s = m % ntm
                b2.free = t = stt(TM[:, s, :], XT[:, m, :], par_col(gain, m), b2.t[:, 0:T], ALU.mult, ALU.mult,
                                  tok, x_tok[m], tm_free[s])
                tm_free[s] = write(m, TM[:, s, :], t)
                toks.append(tm_free[s])
            return toks

        def norm_h(gain, ph, mem=None):
            pe = PE.last
            if mem is None:
                mem = (sb(f"SQ_{gain}", [128, 2, T], F, ph)[:, :, :], sb(f"TM_{gain}", [128, 4, T], F, ph)[:, :, :],
                       [sb(f"sm{i}_{gain}", [128, 2], F, ph)[:, :] for i in range(3)])
            return rmsnorm(gain, *mem, banks[4], banks[5], lambda m, src, t: split(
                src, HH[:, m, :], HL[:, m, :], t, pe, q=G if m % 3 == 2 else V))

        t_x = S.dma(lambda e: e.dma_start(XT[:, :, :], xt), c_x)
        t_par = S.dma(lambda e: e.dma_start(PAR[:, :], par), c_par)
        t_con = S.dma(lambda e: e.dma_start(COM[:, :], con[:, 0:NCOMMON]), c_con)
        G.do(lambda e: e.memset(EPSC[:, :], EPS))
        t_one = G.do(lambda e: e.memset(ONEC[:, :], 1.0))
        for q in (PE, V, A):
            q.wait(t_par, t_con, t_one)
        x_tok = [t_x] * KD

        def constant(name, ph, rows=128):
            o, n = CCOL[name]
            t = sb("c_" + name + str(S.count + len(S.items)), [128, n], F, ph)
            return t[0:rows, :], S.dma(lambda e: e.dma_start(t[0:rows, :], con[0:rows, o:o + n]), c_late)

        with ExitStack() as ph:
            INV, t_inv = constant("invcnt", ph)
            for _ in range(NRAW):
                W.load()
            PAD = T + 16
            H0 = sb("H0", [128, KD, PAD], F, ph)
            PA, PB = sb("PA", [128, KD, PAD], F, ph), sb("PB", [128, KD, PAD], F, ph)
            Y = sb("Y", [128, KD, T], F, ph)
            t_z = G.do(lambda e: e.memset(H0[:, :, 0:16], 0.0))
            SQp, smp = sb("SQp", [128, 4, T], F, ph), [sb(f"smp{i}", [128, 2], F, ph)[:, :] for i in range(3)]
            h_tok = rmsnorm("mix_norm0", SQp[:, :, :], H0[:, :, 16:PAD], smp, banks[4], banks[5],
                            lambda m, src, t: t)
            for _ in range(NSPLIT):
                W.split()
            sums, p_tok = {}, {}
            for g in (3, 0, 1, 2):
                q = G if g == 3 else V
                two = slice(2 * g, 2 * g + 2)
                src, t = H0[:, two, :], [h_tok[2 * g + 1], t_z]
                for step in range(g + 1):
                    sh = 1 << step
                    at = 2 * sh - 1
                    dst = (PA, PB)[step % 2][:, two, :]
                    t = tt(dst[:, :, at:PAD], src[:, :, at:PAD], src[:, :, at - sh:PAD - sh], ALU.add, t, q=q)
                    src = dst
                sums[g] = src, t
            for g in range(4):
                (src, t), w, two = sums[g], 2 << g, slice(2 * g, 2 * g + 2)
                t1 = stt(Y[:, two, :], src[:, :, 16:PAD], 1.0 / w, H0[:, two, 16:PAD], ALU.mult, ALU.subtract, t)
                inv = INV[:, 16 * g:16 * g + w - 1].unsqueeze(1).to_broadcast([128, 2, w - 1])
                t1 = tt(Y[:, two, 0:w - 1], src[:, :, 16:15 + w], inv, ALU.mult, t1, t_inv)
                t1 = tt(Y[:, two, 0:w - 1], Y[:, two, 0:w - 1], H0[:, two, 16:15 + w], ALU.subtract, t1)
                p_tok[g] = split(Y[:, two, :], HH[:, two, :], HL[:, two, :], t1)
            b4 = Pool(banks[4:8])
            for half in range(2):
                wh, wl, wt = W.take("pool", half)
                for g2 in range(2):
                    g = 2 * half + g2
                    for mo in range(2):
                        def wtile(k, base=512 * g2 + 128 * mo):
                            return wh[:, base + 256 * k:base + 256 * k + 128], wl[:, base + 256 * k:base + 256 * k + 128]
                        bank, tok = project_t(b4, 2, wtile, wt, HH[:, 2 * g:2 * g + 2, :], HL[:, 2 * g:2 * g + 2, :],
                                              [p_tok[g]] * 2)
                        m = 2 * g + mo
                        t = ts(Y[:, m, :], bank.t[:, 0:T], par_col("pool_b", m), par_col("pool_scale", m),
                               ALU.add, ALU.mult, tok, p_tok[g])
                        b4.put(bank, t)
                        x_tok[m] = tt(XT[:, m, :], XT[:, m, :], Y[:, m, :], ALU.add, t)
                W.done(tok)

        def ffn(i):
            with ExitStack() as ph:
                h_tok = norm_h(f"ffn_norm{i}", ph)
                main = Pool(banks[4:8])
                C, SI, GG = (sb(f"{n}{i}", [128, 2, T], F, ph) for n in ("C", "SI", "GG"))
                g_tok, acc_tok = [None] * JF, [None] * JF

                def out_block(j):
                    acc_tok[j] = accumulate(f"out{i}", j, GH[:, j % 2, :], GL[:, j % 2, :], g_tok[j], j == 0, j == JF - 1)

                for j in range(JF):
                    s = j % 2
                    gb, g_pe = project_block(main, f"gate{i}", j, HH, HL, h_tok)
                    vb, v_pe = project_block(main, f"val{i}", j, HH, HL, h_tok)
                    if j:
                        out_block(j - 1)
                    before = g_tok[j - 2] if j >= 2 else None
                    cw = [par_col(f"conv{i}", 22 * t + j) for t in range(3)]
                    a1 = act(C[:, s, :], gb.t[:, 0:T], ACT.Identity, g_pe, before,
                             bias=par_col(f"conv_b{i}", j), scale=cw[2])
                    v1 = stt(C[:, s, 1:T], gb.t[:, 0:T - 1], cw[1], C[:, s, 1:T], ALU.mult, ALU.add, a1)
                    v2 = stt(C[:, s, 2:T], gb.t[:, 0:T - 2], cw[0], C[:, s, 2:T], ALU.mult, ALU.add, v1)
                    main.put(gb, v2)
                    a2 = act(SI[:, s, :], C[:, s, :], ACT.Silu, v2)
                    v3 = tt(GG[:, s, :], SI[:, s, :], vb.t[:, 0:T], ALU.mult, a2, v_pe)
                    main.put(vb, v3)
                    g_tok[j] = split(GG[:, s, :], GH[:, s, :], GL[:, s, :], v3, acc_tok[j - 2] if j >= 2 else None)
                out_block(JF - 1)
                sync_all()
            add_accumulated(acc_tok[JF - 1])

        def head_rows(a):
            return slice(64 * a, 64 * a + 64)

        def small_sets(ph, name):
            return [([sb(f"{name}{k}{i}", [128, 2, 8], F, ph) for i in range(3)], sb(f"{name}T{k}", [8, T], F, ph))
                    for k in range(2)]

        small_use = [0]

        def norm_steps(pool, sqs, blk, sel, n, sets, fin, read=None):
            cpc = blk.shape[1]
            w = cpc * len(sqs)
            (small, rt), small_use[0] = sets[small_use[0] % 2], small_use[0] + 1
            while not pool.has():
                yield
            bank = pool.get()
            for i, (sq, t) in enumerate(sqs):
                for k in range(2):
                    tok = mm(bank.t[:, 8 * k + cpc * i:8 * k + cpc * i + cpc], sq[:, c128(k)], blk, True, True,
                             t, bank.free, inc=True)
            if read is not None:
                read(tok)
            yield
            sums = bank.t[:, 0:16].rearrange("p (k c) -> p k c", k=2)[:, :, 0:w]
            tr, free = inverse_root(sums, n, [x[:, :, 0:w] for x in small], tok)
            pool.put(bank, free)
            yield
            while not pool.has():
                yield
            bank = pool.get()
            for k in range(2):
                tok = transpose(bank.t[0:w, c128(k)], small[0][:, k, 0:w], tr, bank.free, inc=(k == 1))
            yield
            tr = vcopy(rt[0:w, :], bank.t[0:w, 0:T], tok, PE.last)
            pool.put(bank, tr)
            yield
            for i0 in range(0, len(sqs), 2):
                while not pool.has():
                    yield
                bank = pool.get()
                mine = range(i0, min(i0 + 2, len(sqs)))
                for i in mine:
                    tok = mm(bank.t[:, T * (i - i0):T * (i - i0) + T], sel[0:w, c128(i)], rt[0:w, :], True, True,
                             tr, bank.free, inc=True)
                yield
                for i in mine:
                    free = fin(i, bank.t[:, T * (i - i0):T * (i - i0) + T], tok)
                pool.put(bank, free)
            yield

        def take_chunk(main, name, idx, dst, sq, h_tok, sq_free):
            bank, tok = project_block(main, name, idx, HH, HL, h_tok)
            t = act(dst, bank.t[:, 0:T], ACT.Copy, tok)
            main.put(bank, t)
            return tt(sq, dst, dst, ALU.mult, t, sq_free, q=G), t

        def start_acc(bg):
            kept = Pool([])
            while len(kept.banks) < 4:
                for b in list(bg.banks):
                    if b in banks[0:4]:
                        bg.banks.remove(b)
                        kept.banks.append(b)
                if len(kept.banks) < 4:
                    tasks.step()

        def until(done):
            while not done():
                tasks.step()

        def attention():
            ph = ExitStack()
            B = sb("B", [128, 16, 384], F, ph)
            t_b = S.dma(lambda e: e.dma_start(B[:, :, :], rel), c_rel)
            BLK2, _ = constant("blk2", ph)
            SEL2, t_c = constant("sel2", ph, 8)
            h_tok = norm_h("mix_norm1", ph)
            Q, K = sb("Q", [128, KD, T], F, ph), sb("K", [128, KD, T], F, ph)
            VN = sb("VN", [128, 2, D], F, ph)
            SS = sb("SS", [128, 16, 384], F, ph)
            SQG = sb("SQG", [128, 4, T], F, ph)
            PT = sb("PT", [128, 16, 384], F, ph)
            AH, AL = sb("AH", [128, KD, T], R, ph), sb("AL", [128, KD, T], R, ph)
            MX, NM, SM, RC = (sb(n, [128, 32], F, ph) for n in ("MX", "NM", "SM", "RC"))
            sets = small_sets(ph, "sa")
            main, bg = Pool(banks[4:8]), Pool(banks[0:4])
            PE.wait(t_c)
            W.on_pool = 3
            tasks.rate = RATE_A
            v_tok = {}
            V.wait(t_b)
            V.do(lambda e: e.memset(B[0:64, :, 64:128], -1e30))
            t_m = V.do(lambda e: e.memset(B[0:64, :, 320:384], -1e30))
            a_tok, sq_free = [None] * KD, [None]
            spans = ((0, 128), (128, 384))

            def pair(m, qk_tok):
                heads = (2 * m, 2 * m + 1)
                while not bg.has(2):
                    yield
                two = [bg.get(), bg.get()]
                toks = []
                for a, h in enumerate(heads):
                    b, r = two[a], head_rows(a)
                    mm(b.t[:, 0:128], Q[r, m, 0:128], K[r, m, 0:128], True, True, b.free, qk_tok)
                    toks.append(mm(b.t[:, 128:384], Q[r, m, 128:256], K[r, m, :], True, True, inc=True))
                yield
                for a, h in enumerate(heads):
                    t = stt(SS[:, h, :], two[a].t[:, 0:384], 0.125, B[:, h, :], ALU.mult, ALU.add, toks[a], t_m)
                    bg.put(two[a], t)
                yield
                for i, (lo, hi) in enumerate(spans):
                    reduce_(MX[:, 4 * m + 2 * i:4 * m + 2 * i + 2], SS[:, 2 * m:2 * m + 2, lo:hi], ALU.max, t)
                t = ts(NM[:, 4 * m:4 * m + 4], MX[:, 4 * m:4 * m + 4], -1.0, None, ALU.mult, None, V.last)
                yield
                for i, (lo, hi) in enumerate(spans):
                    for a, h in enumerate(heads):
                        c = 4 * m + 2 * i + a
                        te = act(SS[:, h, lo:hi], SS[:, h, lo:hi], ACT.Exp, t, bias=NM[:, c:c + 1], accum=SM[:, c:c + 1])
                yield
                t = V.do(lambda e: e.reciprocal(RC[:, 4 * m:4 * m + 4], SM[:, 4 * m:4 * m + 4]), te)
                for i, (lo, hi) in enumerate(spans):
                    for a, h in enumerate(heads):
                        c = 4 * m + 2 * i + a
                        tn = ts(SS[:, h, lo:hi], SS[:, h, lo:hi], RC[:, c:c + 1], None, ALU.mult, None, t)
                yield
                while not bg.has(2):
                    yield
                two = [bg.get(), bg.get()]
                for a, h in enumerate(heads):
                    for i in range(3):
                        toks[a] = transpose(two[a].t[:, c128(i)], SS[:, h, c128(i)], tn, two[a].free, inc=(i == 2))
                yield
                for a, h in enumerate(heads):
                    tp = act(PT[:, h, :], two[a].t[:, 0:384], ACT.Copy, toks[a])
                    bg.put(two[a], tp)
                yield
                while not bg.has() or m // 4 not in v_tok:
                    yield
                ob = bg.get()
                for a, h in enumerate(heads):
                    r, p = head_rows(a), PT[:, h, :]
                    mm(ob.t[r, 0:T], VN[:, 0, 64 * h:64 * h + 64], p[:, 0:T], True, False, tp, v_tok[m // 4], ob.free)
                    tok = mm(ob.t[r, 128:T], VN[:, 1, 64 * h:64 * h + 64], p[:, T:384], False, True, inc=True)
                yield
                th = act(AH[:, m, :], ob.t[:, 0:T], ACT.Copy, tok)
                a_tok[m] = tt(AL[:, m, :], ob.t[:, 0:T], AH[:, m, :].bitcast(F), ALU.subtract, th)
                bg.put(ob, a_tok[m])

            def group(g, sqs, dsts):
                def fin(i, root, tok):
                    gain = "attn_q_norm" if i % 2 == 0 else "attn_k_norm"
                    t = stt(dsts[i], dsts[i], par_col(gain), root, ALU.mult, ALU.mult, tok)
                    if i % 2 == 1:
                        tasks.add(pair(2 * g + i // 2, t))
                    return t
                yield from norm_steps(bg, sqs, BLK2, SEL2, 64, sets, fin, sq_free.append)

            for g in range(4):
                sqs, dsts = [], []
                until(lambda: len(sq_free) > g)
                for i in range(4):
                    m = 2 * g + i // 2
                    dst = (Q, K)[i % 2][:, m, :]
                    t, tc = take_chunk(main, "qk", 8 * (i % 2) + m, dst, SQG[:, i, :], h_tok, sq_free[g])
                    sqs.append((SQG[:, i, :], [t, tc]))
                    dsts.append(dst)
                    if i < 3:
                        tasks.tick()
                tasks.add(group(g, sqs, dsts))
                tasks.tick()
            project_natural(main, "v", VN, D, h_tok, v_tok)
            bg.banks += main.banks
            start_acc(bg)
            for m in range(KD):
                until(lambda: a_tok[m] is not None)
                tok = accumulate("wo", m, AH[:, m, :], AL[:, m, :], a_tok[m], m == 0, m == KD - 1)
                tasks.tick()
            tasks.drain()
            W.on_pool = 0
            sync_all()
            ph.close()
            add_accumulated(tok)

        def mixers():
            ph = ExitStack()
            h_tok = norm_h("norm_attn_2", ph)
            (BLK2, _), (SEL2, _), (SEL1, _) = constant("blk2", ph), constant("sel2", ph, 8), constant("sel1", ph, 8)
            (ROT, _), (TRI, _), (ONES, _), (CEN, _) = (constant(n, ph) for n in ("rot", "tri", "ones", "cen"))
            (DECF, _), (NMASK, _), (CS, _), (SN, t_c) = (constant(n, ph) for n in ("decay", "nmask", "cos", "sin"))
            DEC = DECF.rearrange("p (h c) -> p h c", h=8)
            RQ, RK, SQ_, SK = (sb(n, [128, 4, T], F, ph) for n in ("RQ", "RK", "SQ_", "SK"))
            RV, SV = sb("RV", [128, 2, D], F, ph), sb("SV", [128, 2, 512], F, ph)
            RG, GA, GB = (sb(n, [128, KD, T], F, ph) for n in ("RG", "GA", "GB"))
            SBH, SBL = sb("SBH", [128, 4, T], R, ph), sb("SBL", [128, 4, T], R, ph)
            RTH, RTL = sb("RTH", [128, KD, T], R, ph), sb("RTL", [128, KD, T], R, ph)
            ZS, LS, NS_ = (sb(n, [128, 2, 768], F, ph) for n in ("ZS", "LS", "NS_"))
            SQG = sb("SQG2", [128, 4, T], F, ph)
            RP = sb("RP", [128, 2, T], F, ph)
            sets = small_sets(ph, "sm")
            main, bg = Pool(banks[4:8]), Pool(banks[0:4])
            for q in (PE, V, A):
                q.wait(t_c)
            done = {"stick": 0, "ret": 0, "rg": None}
            slot_free = [None, None]
            sq_free = [None]
            tasks.rate = RATE_M
            rt_tok = [None] * 8
            sb_tok = [None] * 4

            def stick(m, qk_tok, sv_tok):
                s = m % 2
                Z, L, N = (x[:, s, :] for x in (ZS, LS, NS_))
                Z2, L2, N2 = (x.rearrange("p (a c) -> p a c", a=2) for x in (Z, L, N))
                NM2 = NMASK.unsqueeze(1).to_broadcast([128, 2, 384])
                while not bg.has(2) or (m >= 2 and sb_tok[m - 2] is None):
                    yield
                two, toks = [bg.get(), bg.get()], [None, None]
                for a in range(2):
                    b, r = two[a], head_rows(a)
                    mm(b.t[:, 0:T], SK[r, m, 0:128], SQ_[r, m, :], True, True, b.free, qk_tok)
                    toks[a] = mm(b.t[:, T:384], SK[r, m, 128:T], SQ_[r, m, 128:T], True, True, inc=True)
                yield
                for a in range(2):
                    t = act(Z2[:, a, :], two[a].t[:, 0:384], ACT.Copy, toks[a], slot_free[s], scale=0.125)
                    bg.put(two[a], t)
                yield
                t = act(L, Z, ACT.Abs, t)
                t = act(L, L, ACT.Exp, t, scale=-1.0)
                t = act(L, L, ACT.Ln, t, bias=ONEC[:, :])
                yield
                stt(N, Z, 0.0, L, ALU.max, ALU.add, t, slot_free[s])
                tn = tt(N2, N2, NM2, ALU.mult, V.last)
                yield
                tz = stt(Z, Z, 0.0, L, ALU.min, ALU.subtract, tn)
                while not bg.has(2):
                    yield
                two = [bg.get(), bg.get()]
                for a in range(2):
                    b = two[a]
                    mm(b.t[:, 0:T], TRI, N2[:, a, 0:T], True, False, b.free, tn)
                    mm(b.t[:, 128:T], ONES, N2[:, a, T:384], False, False)
                    toks[a] = mm(b.t[:, T:384], TRI, N2[:, a, T:384], False, True, inc=True)
                yield
                for a in range(2):
                    t = tt(Z2[:, a, :], Z2[:, a, :], two[a].t[:, 0:384], ALU.add, toks[a], tz)
                    bg.put(two[a], t)
                yield
                t = act(L, Z, ACT.Exp, t)
                yield
                t = stt(L2, L2, -1.0, NM2, ALU.mult, ALU.mult, t)
                yield
                while not bg.has():
                    yield
                ob = bg.get()
                for a in range(2):
                    h, r = 2 * m + a, head_rows(a)
                    mm(ob.t[r, 0:T], SV[:, 0, 64 * h:64 * h + 64], L2[:, a, 0:T], True, False, t, sv_tok, ob.free)
                    tok = mm(ob.t[r, 128:T], SV[:, 1, 64 * h:64 * h + 64], L2[:, a, T:384], False, True, inc=True)
                slot_free[s] = tok
                yield
                th = act(SBH[:, m, :], ob.t[:, 0:T], ACT.Copy, tok)
                sb_tok[m] = tt(SBL[:, m, :], ob.t[:, 0:T], SBH[:, m, :].bitcast(F), ALU.subtract, th)
                bg.put(ob, sb_tok[m])
                done["stick"] += 1

            def retention(m, qk_tok, rv_tok):
                s = m % 2
                ST, Y, YQ = ZS[:, s, :], LS[:, s, 0:512], NS_[:, s, 0:512]
                ST2, Y2, YQ2 = ST.rearrange("p (a c) -> p a c", a=2), Y.rearrange("p (a c) -> p a c", a=2), YQ.rearrange("p (a c) -> p a c", a=2)
                while not bg.has(2) or done["stick"] < 4 or (m >= 2 and done["ret"] < m - 1):
                    yield
                two, toks = [bg.get(), bg.get()], [None, None]
                for a in range(2):
                    b, r = two[a], head_rows(a)
                    mm(b.t[:, 0:T], RK[r, m, 0:128], RQ[r, m, :], True, True, b.free, qk_tok)
                    toks[a] = mm(b.t[:, T:384], RK[r, m, 128:T], RQ[r, m, 128:T], True, True, inc=True)
                yield
                for a in range(2):
                    t = tt(ST2[:, a, :], two[a].t[:, 0:384], DEC[:, 2 * m + a, :], ALU.mult, toks[a], slot_free[s])
                    bg.put(two[a], t)
                yield
                while not bg.has():
                    yield
                b = bg.get()
                for a in range(2):
                    h, o = 2 * m + a, T * a
                    mm(b.t[:, o:o + T], RV[:, 0, c128(h)], ST2[:, a, 0:T], True, False, t, rv_tok, b.free)
                    tok = mm(b.t[:, o + 128:o + T], RV[:, 1, c128(h)], ST2[:, a, T:384], False, True, inc=True)
                yield
                t = act(Y, b.t[:, :], ACT.Copy, tok, slot_free[s])
                bg.put(b, t)
                yield
                while not bg.has():
                    yield
                b = bg.get()
                tok = mm(b.t[:, :], CEN, Y, True, True, t, b.free, inc=True)
                yield
                t = act(Y, b.t[:, :], ACT.Copy, tok)
                bg.put(b, t)
                t2 = tt(YQ, Y, Y, ALU.mult, t, slot_free[s], q=G)
                yield
                out_tok = {}

                def fin(i, root, tok):
                    out_tok[i] = stt(Y2[:, i, :], Y2[:, i, :], par_col("group_norm", 2 * m + i), root, ALU.mult,
                                     ALU.mult, tok)
                    return out_tok[i]
                yield from norm_steps(bg, [(YQ2[:, a, :], [t2, t]) for a in range(2)], ONE, SEL1, 128, sets, fin)
                while done["rg"] is None:
                    yield
                for a in range(2):
                    h = 2 * m + a
                    t = tt(Y2[:, a, :], Y2[:, a, :], RG[:, h, :], ALU.mult, done["rg"], out_tok[a])
                    rt_tok[h] = split(Y2[:, a, :], RTH[:, h, :], RTL[:, h, :], t)
                slot_free[s] = rt_tok[2 * m + 1]
                done["ret"] += 1

            def group(kind, g, sqs, dsts, v_tok):
                def fin(i, root, tok):
                    gain = f"{kind}_{'q' if i % 2 == 0 else 'k'}_norm"
                    t = stt(dsts[i], dsts[i], par_col(gain), root, ALU.mult, ALU.mult, tok)
                    if kind == "sb" and i % 2 == 1:
                        tasks.add(stick(2 * g + i // 2, t, v_tok))
                    return t
                yield from norm_steps(bg, sqs, BLK2, SEL2, 64, sets, fin, sq_free.append)
                if kind == "sb":
                    return
                t = V.last
                for i in range(4):
                    while not bg.has():
                        yield
                    b = bg.get()
                    tok = mm(b.t[:, 0:T], ROT, dsts[i], True, True, t, b.free, inc=True)
                    yield
                    r = RP[:, i % 2, :]
                    tr = tt(r, b.t[:, 0:T], SN, ALU.mult, tok, V.last)
                    bg.put(b, tr)
                    tt(dsts[i], dsts[i], CS, ALU.mult, tok)
                    tk = tt(dsts[i], dsts[i], r, ALU.add, V.last)
                    if i % 2 == 1:
                        tasks.add(retention(2 * g + i // 2, tk, v_tok))

            def two_groups(kind, name, dq, dk, v_tok):
                for g in range(2):
                    sqs, dsts = [], []
                    group_no = 2 * (kind == "ret") + g
                    until(lambda: len(sq_free) > group_no)
                    for i in range(4):
                        m = 2 * g + i // 2
                        dst = (dq, dk)[i % 2][:, m, :]
                        t, tc = take_chunk(main, name, 4 * (i % 2) + m, dst, SQG[:, i, :], h_tok, sq_free[group_no])
                        sqs.append((SQG[:, i, :], [t, tc]))
                        dsts.append(dst)
                        if i < 3:
                            tasks.tick()
                    tasks.add(group(kind, g, sqs, dsts, v_tok))
                    tasks.tick()

            def gates(name, dst):
                for m in range(KD):
                    bank, tok = project_block(main, name, m, HH, HL, h_tok)
                    t = act(dst[:, m, :], bank.t[:, 0:T], ACT.Copy, tok)
                    main.put(bank, t)
                    tasks.tick()
                return t

            sv_tok = project_natural(main, "sv", SV, 512, h_tok)
            two_groups("sb", "sqk", SQ_, SK, sv_tok)
            rv_tok = project_natural(main, "rv", RV, D, h_tok)
            two_groups("ret", "rqk", RQ, RK, rv_tok)
            t = gates("rg", RG)
            for k in range(2):
                t = act(RG[:, 4 * k:4 * k + 4, :], RG[:, 4 * k:4 * k + 4, :], ACT.Silu, t)
            done["rg"] = t
            gates("ga", GA)
            t = gates("gb", GB)
            for k in range(2):
                act(GA[:, 4 * k:4 * k + 4, :], GA[:, 4 * k:4 * k + 4, :], ACT.Sigmoid, t)
                gb_tok = act(GB[:, 4 * k:4 * k + 4, :], GB[:, 4 * k:4 * k + 4, :], ACT.Sigmoid, t)
            until(lambda: done["stick"] == 4)
            for b in range(4):
                wh, wl, wt = W.take("sbbr", b)
                for g in range(2):
                    m = 2 * b + g

                    def wtile(k, base=512 * g):
                        return wh[:, base + 128 * k:base + 128 * k + 128], wl[:, base + 128 * k:base + 128 * k + 128]

                    bank, tok = project_t(main, 4, wtile, wt, SBH, SBL, sb_tok)
                    t = tt(GB[:, m, :], GB[:, m, :], bank.t[:, 0:T], ALU.mult, tok, gb_tok)
                    main.put(bank, t)
                W.done(tok)
                tasks.tick()
            until(lambda: done["ret"] == 4)
            tasks.drain()
            start_acc(bg)
            g_tok, acc_tok = [None] * KD, [None] * KD
            for m in range(KD):
                s = m % 2
                bank, tok = project_block(main, "rbr", m, RTH, RTL, rt_tok)
                t = tt(RP[:, s, :], GA[:, m, :], bank.t[:, 0:T], ALU.mult, tok, gb_tok, g_tok[m - 2] if m >= 2 else V.last)
                main.put(bank, t)
                t = tt(RP[:, s, :], RP[:, s, :], GB[:, m, :], ALU.add, t)
                g_tok[m] = split(RP[:, s, :], GH[:, s, :], GL[:, s, :], t, acc_tok[m - 2] if m >= 2 else None)
                if m:
                    acc_tok[m - 1] = accumulate("wout", m - 1, GH[:, 1 - s, :], GL[:, 1 - s, :], g_tok[m - 1], m == 1, False)
            tok = accumulate("wout", 7, GH[:, 1, :], GL[:, 1, :], g_tok[7], False, True)
            sync_all()
            ph.close()
            add_accumulated(tok)

        def peer():
            ph = ExitStack()
            IOTA, t_io = constant("iota", ph)
            BIG = sb("BIG", [128, 128 * T], F, ph)
            BIG3 = BIG[:, :].rearrange("p (c t) -> p c t", t=T)
            RB = sb("RB", [128, 5, T], B16, ph)
            IREP = sb("IREP", [128, 128, 8], B16, ph)
            GT_ = sb("GT_", [128, 2, T], F, ph)
            OX = sb("OX", [128, 1024], B16, ph)
            XB = XT[:, :, :].rearrange("p k t -> p (k t)").bitcast(B16)
            O1, O2, P1, P2 = (XB[:, 1024 * k:1024 * k + 1024].rearrange("p (i t) -> p i t", t=8) for k in range(4))
            P3 = OX[:, :].rearrange("p (i t) -> p i t", t=8)
            at = [128 * T]

            def scratch(m, n):
                at[0] -= m * n
                return BIG[:, at[0]:at[0] + m * n].rearrange("p (m n) -> p m n", n=n)

            KEY = scratch(2, 128)
            t_key = S.dma(lambda e: e.dma_start(KEY, keys), c_key)
            QT = scratch(16, T)
            SC_ = [scratch(16, 128), scratch(16, 128)]
            I1F, I2F, GT = (scratch(8, 16) for _ in range(3))
            S2 = scratch(1, 256)[:, 0, :]
            TV = scratch(16, 16)
            TI = scratch(16, 16).bitcast(U32)
            CV = scratch(8, 16)
            CI, AB = scratch(8, 16).bitcast(U32), scratch(8, 16).bitcast(U32)
            AF = scratch(8, 16)
            IF = scratch(16, 16)
            CAND, OH = scratch(1, 2048)[:, 0, :], scratch(1, 2048)[:, 0, :]
            SMX = scratch(1, 8)[:, 0, :]
            NSQ, NTM = scratch(2, T), scratch(4, T)
            smp = [scratch(1, 8)[:, 0, 0:2] for _ in range(3)]
            lowest = at[0] // T
            SC4 = CAND.rearrange("p (h a b) -> p h a b", h=8, a=16)
            OH4 = OH.rearrange("p (h a b) -> p h a b", h=8, a=16)
            h_tok = norm_h("norm_ffn_2", ph, (NSQ, NTM, smp))
            for m in range(KD):
                x_pe = mm(acc_view(m), IDENT, XT[:, m, :], m % 2 == 0, False, x_tok[m], banks[m // 2].free,
                          inc=(m == KD - 1))
            V.wait(t_io)
            t_irep = vcopy(IREP[:, :, :], IOTA.unsqueeze(2).to_broadcast([128, 128, 8]))
            main, bg = Pool(banks[4:6]), Pool(banks[6:8])
            W.on_pool = POOL_PEER
            tasks.rate = RATE_R
            s_tok = {}
            r_done = []

            def scores(q4, q_tok):
                for t_ in range(2):
                    while not bg.has():
                        yield
                    bank = bg.get()
                    for l in range(4 * q4, 4 * q4 + 4):
                        tok = mm(bank.t[:, c128(l % 4)], QT[:, l, c128(t_)], KEY[:, l % 2, :], True, True,
                                 q_tok, t_key, bank.free, inc=(l % 4 == 3))
                    yield
                    t = act(SC_[t_][:, 4 * q4:4 * q4 + 4, :], bank.t[:, :].rearrange("p (a b) -> p a b", b=128),
                            ACT.Copy, tok)
                    bg.put(bank, t)
                    s_tok[t_, q4] = t

            def top16(src, work_, vals, idx, tok):
                V.do(lambda e: e.max(vals[:, 0:8], src), tok, V.last)
                V.do(lambda e: e.max_index(idx[:, 0:8], vals[:, 0:8], src), V.last)
                V.do(lambda e: e.match_replace(work_, vals[:, 0:8], src, NEG), V.last)
                V.do(lambda e: e.max(vals[:, 8:16], work_), V.last)
                return V.do(lambda e: e.max_index(idx[:, 8:16], vals[:, 8:16], work_), V.last)

            def bc(ap, axis):
                return ap.unsqueeze(axis).to_broadcast([128, 8, 16, 16])

            def route():
                for t_ in range(2):
                    for l in range(16):
                        while (t_, l // 4) not in s_tok:
                            yield
                        top16(SC_[t_][:, l, :], S2[:, 0:128], TV[:, l, :], TI[:, l, :], s_tok[t_, l // 4])
                        yield
                    TVh = TV.rearrange("p (h s) k -> p h s k", s=2)
                    tt(SC4, bc(TVh[:, :, 0, :], 3), bc(TVh[:, :, 1, :], 2), ALU.add, V.last)
                    yield
                    for h in range(8):
                        top16(CAND[:, 256 * h:256 * h + 256], S2, CV[:, h, :], CI[:, h, :], V.last)
                        yield
                    vcopy(IF, TI, V.last)
                    IFh = IF.rearrange("p (h s) k -> p h s k", s=2)
                    for side, dst in ((0, I1F), (1, I2F)):
                        if side == 0:
                            V.do(lambda e: e.tensor_scalar(AB, CI, 4, None, ALU.logical_shift_right), V.last)
                        else:
                            V.do(lambda e: e.tensor_scalar(AB, CI, 15, None, ALU.bitwise_and), V.last)
                        vcopy(AF, AB, V.last)
                        i16 = IOTA[:, 0:16].unsqueeze(1).unsqueeze(1).to_broadcast([128, 8, 16, 16])
                        tt(OH4, bc(AF, 3), i16, ALU.is_equal, V.last)
                        yield
                        tt(OH4, OH4, bc(IFh[:, :, side, :], 2), ALU.mult, V.last)
                        yield
                        reduce_(dst, OH4, ALU.add, V.last)
                        yield
                    t = tt(GT, CV, CV[:, :, 0:1].to_broadcast([128, 8, 16]), ALU.subtract, V.last)
                    t = act(GT, GT, ACT.Exp, t)
                    yield
                    reduce_(SMX, GT, ALU.add, t)
                    V.do(lambda e: e.reciprocal(SMX, SMX), V.last)
                    t = tt(GT, GT, SMX.unsqueeze(2).to_broadcast([128, 8, 16]), ALU.mult, V.last)
                    while not bg.has():
                        yield
                    bank = bg.get()
                    for i, src in enumerate((I1F, I2F, GT)):
                        tok = transpose(bank.t[:, c128(i)], src.rearrange("p a b -> p (a b)"), t, bank.free, inc=(i == 2))
                    yield
                    cols = c128(t_)
                    vcopy(RB[:, 0:2, cols], bank.t[:, 0:T].rearrange("p (a b) -> p a b", b=128), tok)
                    t = vcopy(GT_[:, 0, cols], bank.t[:, T:384], tok)
                    bg.put(bank, t)
                    vcopy(RB[:, 2, cols], GT_[:, 0, cols], t)
                    tt(GT_[:, 1, cols], GT_[:, 0, cols], RB[:, 2, cols], ALU.subtract, V.last)
                    vcopy(RB[:, 3, cols], GT_[:, 1, cols], V.last)
                    tt(GT_[:, 1, cols], GT_[:, 1, cols], RB[:, 3, cols], ALU.subtract, V.last)
                    r_tok[0] = vcopy(RB[:, 4, cols], GT_[:, 1, cols], V.last)
                    yield
                r_done.append(1)

            r_tok = [None]
            tokens_done = [0]
            chunks_done = [0]
            slot_tok, gelu_tok = [None], [None]

            meets = []

            def meet(k):
                q, two, toks = meets[0]
                n, lo = chunks_done[0], 8 * q + 4 * k
                src = two[k].t[:, :].rearrange("p (t c) -> p c t", t=4)
                dst = BIG3[:, :, lo:lo + 4]
                tm = tt(dst[:, 0:n, :], dst[:, 0:n, :], src[:, 0:n, :], ALU.mult, toks[k], gelu_tok[0])
                if n < 128:
                    tm = act(dst[:, n:128, :], src[:, n:128, :], ACT.Copy, tm, slot_tok[0])
                bg.put(two[k], tm)
                slot_tok[0] = tm
                tokens_done[0] = lo + 4
                if k:
                    meets.pop(0)

            def gates():
                while not r_done:
                    yield
                o_free = x_pe
                for q in range(T // 8):
                    sl = slice(8 * q, 8 * q + 8)

                    def row(i):
                        return RB[:, i, sl].unsqueeze(1).to_broadcast([128, 128, 8])

                    tt(O1, row(0), IREP[:, :, :], ALU.is_equal, r_tok[0], o_free)
                    t2 = tt(O2, row(1), IREP[:, :, :], ALU.is_equal)
                    yield
                    t3 = tt(P3, O2, row(4), ALU.mult, t2, o_free, q=G)
                    for i, P in enumerate((P1, P2)):
                        t = tt(P, O2, row(2 + i), ALU.mult, t2)
                    yield
                    if meets:
                        meet(0)
                    yield
                    if meets:
                        meet(1)
                    yield
                    while not bg.has(2):
                        yield
                    two = [bg.get(), bg.get()]
                    toks = [None, None]
                    for k in range(8):
                        b = two[k // 4]
                        for i, P in enumerate((P1, P2, P3)):
                            tok = mm(b.t[:, c128(k % 4)], O1[:, :, k], P[:, :, k], i == 0 and k % 4 == 0, i == 2,
                                     t, t3, b.free, inc=(i == 2 and k % 4 == 3))
                        if k == 3:
                            toks[0] = tok
                            yield
                    toks[1] = o_free = tok
                    meets.append((q, two, toks))
                    yield
                while meets:
                    meet(0)
                    yield
                    meet(1)
                    yield

            for l in range(16):
                bank, tok = project_block(main, "pq", l, HH, HL, h_tok)
                q_tok = act(QT[:, l, :], bank.t[:, 0:T], ACT.Copy, tok)
                main.put(bank, q_tok)
                if l % 4 == 3:
                    tasks.add(scores(l // 4, q_tok))
                if l == 3:
                    tasks.add(route())
                    tasks.add(gates())
                tasks.tick()
            for c in range(128):
                if c == lowest and not r_done:
                    until(lambda: r_done)
                if c == lowest:
                    A.wait(V.last, PE.last)
                bank, tok = project_block(main, "u", c, HH, HL, h_tok)
                tasks.rate = RATE_R if not r_done else RATE_G
                tasks.tick()
                n = tokens_done[0]
                if n < T:
                    t = act(BIG3[:, c, n:T], bank.t[:, n:T], ACT.Gelu_apprx_tanh, tok)
                if n:
                    tmp = GT_[:, c % 2, 0:n]
                    tg = act(tmp, bank.t[:, 0:n], ACT.Gelu_apprx_tanh, tok, gelu_free[c % 2] or V.last)
                    t = tg
                    gelu_free[c % 2] = tt(BIG3[:, c, 0:n], BIG3[:, c, 0:n], tmp, ALU.mult, tg, slot_tok[0])
                main.put(bank, t)
                gelu_tok[0] = t
                chunks_done[0] = c + 1
            tasks.drain()
            W.on_pool = 0
            t_a = [V.last, A.last, slot_tok[0]]
            acc_tok, a_split = [None] * 128, [None] * 128
            for c in range(128):
                s = c % 2
                a_split[c] = split(BIG3[:, c, :], GH[:, s, :], GL[:, s, :], t_a, acc_tok[c - 2] if c >= 2 else None)
                if c:
                    acc_tok[c - 1] = accumulate("w", c - 1, GH[:, 1 - s, :], GL[:, 1 - s, :], a_split[c - 1], False, False)
            tok = accumulate("w", 127, GH[:, 1, :], GL[:, 1, :], a_split[127], False, True)
            for m in range(KD):
                x_tok[m] = vcopy(XT[:, m, :], acc_view(m), tok)
            ph.close()

        gelu_free = [None, None]
        if upto >= 1:
            ffn(0)
        if upto >= 2:
            attention()
        if upto >= 3:
            ffn(1)
        if upto >= 4:
            mixers()
        if upto >= 5:
            peer()
        for c in c_raw:
            S.wait((c[0], c[1]))
        for k in range(4):
            t_o = S.dma(lambda e, k=k: e.dma_start(out[:, 2 * k:2 * k + 2, :], XT[:, 2 * k:2 * k + 2, :]), c_out,
                        x_tok[2 * k], x_tok[2 * k + 1])
        S.wait(t_o)

        block = ctx.enter_context(nc.Block())

        @block.sync
        def _(e):
            S.replay(e)

        @block.scalar
        def _(e):
            A.replay(e)

        @block.vector
        def _(e):
            V.replay(e)

        @block.gpsimd
        def _(e):
            G.replay(e)

        @block.tensor
        def _(e):
            PE.replay(e)
        return W.order


def _vec(v):
    return v.reshape(-1, 128).T


def _cols(w):
    k, n = w.shape
    return w.reshape(k // 128, 128, n // 128, 128).transpose(2, 1, 0, 3).reshape(n // 128, 128, k)


def _natural(w):
    k, n = w.shape
    return w.reshape(4, 2, 128, n // 512, 512).transpose(3, 0, 2, 1, 4).reshape(-1, 128, BLK)


def _wall(i, order):
    wi = i["w_in_2"][0]
    parts = {
        "pool": i["pool_w"][0].reshape(2, 2, 2, 128, 256).transpose(0, 3, 1, 2, 4).reshape(2, 128, BLK),
        "qk": _cols(i["attn_wqkv"][0][:, 0:2048]),
        "v": _natural(i["attn_wqkv"][0][:, 2048:3072]),
        "wo": i["attn_wo"][0].reshape(8, 128, D),
        "rqk": _cols(wi[:, 0:1024]),
        "rv": _natural(wi[:, 1024:2048]),
        "rg": _cols(wi[:, 2048:3072]),
        "sqk": _cols(wi[:, 3072:4096]),
        "sv": _natural(wi[:, 4096:4608]),
        "ga": _cols(wi[:, 4608:5632]),
        "gb": _cols(wi[:, 5632:6656]),
        "sbbr": _cols(i["w_branch_sb_2"][0]).reshape(4, 2, 128, 512).transpose(0, 2, 1, 3).reshape(4, 128, BLK),
        "rbr": _cols(i["w_branch_ret_2"][0]),
        "wout": i["w_out_2"][0].reshape(8, 128, D),
        "pq": _cols(i["peer_w_q_2"][0]),
        "u": i["peer_u_2"][0].reshape(128, 128, 8, 128).transpose(1, 3, 2, 0).reshape(128, 128, BLK),
        "w": i["peer_v_2"][0].reshape(128, 128, D).transpose(1, 0, 2),
    }
    for l in range(2):
        parts[f"gate{l}"] = _cols(i["ffn_w_gate"][l])
        parts[f"val{l}"] = _cols(i["ffn_w_val"][l])
        parts[f"out{l}"] = i["ffn_w_out"][l].reshape(JF, 128, D)
    w = np.empty((N_BLOCKS, 128, BLK), np.float32)
    for at, (name, idx) in enumerate(order):
        w[at] = parts[name][idx]
    w[len(order):] = 0.0
    return w


def _params(i):
    def two(v):
        return np.concatenate([v, v]).reshape(128, 1)

    cols = [_vec(i["mix_norm"][0]), _vec(i["mix_norm"][1]), _vec(i["ffn_norm"][0]), _vec(i["ffn_norm"][1]),
            _vec(i["pool_b"][0]), _vec(i["pool_scale"][0]), two(i["attn_q_norm"][0]), two(i["attn_k_norm"][0])]
    cols += [_vec(i["ffn_conv_w"][l].reshape(-1)) for l in range(2)]
    cols += [_vec(i["ffn_conv_b"][l]) for l in range(2)]
    cols += [_vec(i["norm_attn_2"][0]), two(i["ret_q_norm_2"][0]), two(i["ret_k_norm_2"][0]),
             _vec(i["ret_group_norm_2"][0]), two(i["sb_q_norm_2"][0]), two(i["sb_k_norm_2"][0]),
             _vec(i["norm_ffn_2"][0])]
    return np.ascontiguousarray(np.concatenate(cols, axis=1))


def _relative(table):
    q = np.arange(128)[:, None]
    at = np.concatenate([256 + q - np.arange(128)[None, :], 384 + q - np.arange(T)[None, :]], axis=1)
    return np.ascontiguousarray(table[:, at].transpose(1, 0, 2))


def _constants():
    c = np.zeros((128, NCON), np.float32)

    def put(name, v):
        o, n = CCOL[name]
        c[:, o:o + n] = v

    p = np.arange(128)
    t = np.arange(T)
    same = p[:, None] // 64 == p[None, :] // 64
    k, m = p[:, None] % 64, p[None, :] % 64
    put("ident", np.eye(128))
    put("one", 1.0)
    put("ones", 1.0)
    put("blk2", p[:, None] // 64 == np.arange(2)[None, :])
    col = np.arange(512)[None, :]
    put("sel2", p[:, None] == 2 * (col // 128) + col % 128 // 64)
    put("sel1", p[:, None] == col // 128)
    put("rot", same * (1.0 * (k == m - 32) - 1.0 * (k == m + 32)))
    put("tri", p[:, None] > p[None, :])
    put("cen", np.eye(128) - 1.0 / 128)
    put("iota", p[None, :])
    inv = np.zeros(64)
    for g in range(4):
        inv[16 * g:16 * g + 16] = 1.0 / np.minimum(np.arange(16) + 1, 2 << g)
    put("invcnt", inv[None, :])
    qpos = np.concatenate([t, t[128:]])[None, :]
    kpos = p[:, None] + np.concatenate([np.zeros(T), np.full(128, 128)])[None, :]
    diff = qpos - kpos
    put("decay", np.concatenate([np.where(diff >= 0, np.exp(np.log1p(-np.exp2(-5.0 - h)) * np.maximum(diff, 0)), 0.0)
                                 * 0.125 for h in range(8)], axis=1))
    freqs = (10000.0 ** (-np.arange(32, dtype=np.float32) / 32)).astype(np.float32)
    ang = (t[None, :].astype(np.float32) * freqs[p % 32][:, None]).astype(np.float32).astype(np.float64)
    put("cos", np.cos(ang))
    put("sin", np.sin(ang))
    put("nmask", -1.0 * (diff > 0))
    return c


def kernel(**inputs):
    import concourse.bacc as bacc
    from concourse.bass_utils import run_bass_kernel_spmd

    i = {n: np.asarray(a) for n, a in inputs.items()}
    arrays = {
        "wall": (N_BLOCKS, 128, BLK),
        "par": _params(i),
        "con": _constants(),
        "xt": np.ascontiguousarray(i["x"][0].reshape(T, KD, 128).transpose(2, 1, 0)),
        "rel": _relative(i["attn_rel_bias"][0]),
        "keys": np.ascontiguousarray(np.stack([i["peer_sub_keys_1_2"][0].T, i["peer_sub_keys_2_2"][0].T], axis=1)),
    }
    nc = bacc.Bacc("TRN2", target_bir_lowering=False, num_devices=1)
    args = [nc.dram_tensor(n, a if n == "wall" else a.shape, F, kind="ExternalInput").ap() for n, a in arrays.items()]
    out = nc.dram_tensor("out", (128, KD, T), F, kind="ExternalOutput").ap()
    order = build(nc, *args, out)
    arrays["wall"] = _wall(i, order)
    r = run_bass_kernel_spmd(nc, [arrays], core_ids=[0])
    got = r.results[0]["out"]
    return np.ascontiguousarray(got.transpose(2, 1, 0)).reshape(1, T, D)
```

```python
import math
from contextlib import ExitStack

import numpy as np

import concourse.bass as bass
from concourse import mybir

F = mybir.dt.float32
R = mybir.dt.float32r
U32 = mybir.dt.uint32
B16 = mybir.dt.bfloat16
ALU = mybir.AluOpType
ACT = mybir.ActivationFunctionType
AX = mybir.AxisListType.X
OWN_TABLE = (ACT.Exp, ACT.Ln, ACT.Silu, ACT.Sigmoid, ACT.Gelu_apprx_tanh)

T = 256
D = 1024
KD = D // 128
FF = 2816
JF = FF // 128
EPS = 1e-6
NRAW = 4
NSPLIT = 3
BLK = 1024
N_POOL, N_FFN, N_ATT = 2, 3 * JF, 32
N_IN, N_BR, N_PQ = 52, 20, 16
N_BLOCKS = N_POOL + 2 * N_FFN + N_ATT + N_IN + N_BR + N_PQ + 256
NEG = -3.4028234663852886e38
HOP = 0.2
OWN_HOP = 0.1
AHEAD_F = 1.0, 1.0
AHEAD_A = 0.5, 0.3
AHEAD_M = 0.8, 0.8
AHEAD_P = 1.0, 1.0
POOL_ROUTE, POOL_PEER = 1, 2

_PARAMS = [("mix_norm0", 8), ("mix_norm1", 8), ("ffn_norm0", 8), ("ffn_norm1", 8), ("pool_b", 8),
           ("pool_scale", 8), ("attn_q_norm", 1), ("attn_k_norm", 1), ("conv0", 66), ("conv1", 66),
           ("conv_b0", 22), ("conv_b1", 22), ("norm_attn_2", 8), ("ret_q_norm", 1), ("ret_k_norm", 1),
           ("group_norm", 8), ("sb_q_norm", 1), ("sb_k_norm", 1), ("norm_ffn_2", 8)]
PCOL = {}
NPAR = 0
for _n, _w in _PARAMS:
    PCOL[_n] = NPAR
    NPAR += _w

CCOL = {}
NCON = 0
for _n, _w in [("ident", 128), ("one", 1), ("blk2", 2), ("sel2", 512), ("rot", 128), ("tri", 128), ("ones", 128),
               ("cen", 128), ("sel1", 512), ("decay", 3072), ("nmask", 384), ("cos", 256), ("sin", 256),
               ("invcnt", 64), ("iota", 128)]:
    CCOL[_n] = (NCON, _w)
    NCON += _w
NCOMMON = 129


ABOUT = {}


def columns(ap):
    n = 1
    for d in ap.shape[1:]:
        n *= d
    return n


class Queue:

    def __init__(self, sem):
        self.sem, self.count, self.items, self.seen = sem, 0, [], {}
        self.now, self.set = 0.0, None

    def wait(self, *toks):
        for t in toks:
            if t is None:
                continue
            if isinstance(t, list):
                self.wait(*t)
                continue
            sem, val = t
            self.now = max(self.now, ABOUT.get((sem.name, val), 0.0) + (OWN_HOP if sem is self.sem else HOP))
            if val and self.seen.get(sem.name, 0) < val:
                self.seen[sem.name] = val
                self.items.append(("w", sem, val))

    def do(self, fn, *toks, inc=True, us=0.1):
        self.wait(*toks)
        self.now += us
        if inc:
            ABOUT[self.sem.name, self.count + 1] = self.now
        if inc:
            self.count += 1
        self.items.append(("i", fn, (self.sem, 1) if inc else None))
        return (self.sem, self.count)

    def dma(self, fn, chan, *toks):
        self.wait(*toks)
        self.now += 1.5
        chan[1] += 16
        ABOUT[chan[0].name, chan[1]] = self.now + 2.0
        self.items.append(("i", fn, (chan[0], 16)))
        return (chan[0], chan[1])

    @property
    def last(self):
        return (self.sem, self.count)

    def replay(self, eng):
        for kind, a, b in self.items:
            if kind == "w":
                eng.wait_ge(a, b)
            else:
                ins = a(eng)
                if b:
                    ins.then_inc(*b)


class Bank:
    def __init__(self, t):
        self.t, self.free = t, None


class Pool:

    def __init__(self, banks):
        self.banks = list(banks)

    def has(self, n=1):
        return len(self.banks) >= n

    def get(self):
        return self.banks.pop(0)

    def put(self, bank, tok):
        bank.free = tok
        self.banks.append(bank)


class Tasks:

    def __init__(self, pe, others):
        self.live, self.pe, self.others = [], pe, others
        self.slack, self.lead = AHEAD_F
        ABOUT.clear()
        self.ready = {}

    def add(self, gen):
        self.live.append(gen)

    def advance(self, g):
        before = [q.count for q in (self.pe, *self.others)]
        try:
            next(g)
        except StopIteration:
            self.live.remove(g)
            return
        used = [q.now for q, n in zip((self.pe, *self.others), before) if q.count != n]
        if used:
            self.ready[id(g)] = max(used)

    def step(self):
        for g in list(self.live):
            self.advance(g)

    def tick(self):
        for g in list(self.live):
            if self.ready.get(id(g), 0.0) <= self.pe.now + self.lead and all(
                    q.now <= self.pe.now + self.lead + self.slack for q in self.others):
                self.advance(g)

    def drain(self):
        while self.live:
            self.step()


def build(nc, wall, par, con, xt, rel, keys, out, upto=99):
    ctx = ExitStack()
    with ctx:
        def sb(name, shape, dt=F, where=None):
            return (where or ctx).enter_context(nc.sbuf_tensor(name, shape, dt))

        def sem(name):
            return ctx.enter_context(nc.semaphore(name))

        XT = sb("XT", [128, KD, T])
        HH = sb("HH", [128, KD, T], R)
        HL = sb("HL", [128, KD, T], R)
        GH = sb("GH", [128, 2, T], R)
        GL = sb("GL", [128, 2, T], R)
        RAW = sb("RAW", [128, NRAW, BLK])
        WH = sb("WH", [128, NSPLIT, BLK], R)
        WL = sb("WL", [128, NSPLIT, BLK], R)
        PAR = sb("PAR", [128, NPAR])
        COM = sb("COM", [128, NCOMMON])
        NHALF = sb("NHALF", [128, 2, 8])
        ONEC = sb("ONEC", [128, 1])
        RN = sb("RN", [128, T])
        SM = [sb(f"SM{i}", [128, 2]) for i in range(3)]
        banks = [Bank(ctx.enter_context(nc.psum_tensor(f"ps{i}", [128, 512], F))) for i in range(8)]

        PE, V, A, G, S = (Queue(sem(n)) for n in ("s_pe", "s_dve", "s_act", "s_pool", "s_sp"))
        c_par, c_con, c_late, c_mid, c_key, c_out = ([sem(n), 0] for n in (
            "d_par", "d_con", "d_late", "d_mid", "d_key", "d_out"))
        c_x = [[sem(f"d_x{i}"), 0] for i in range(4)]
        c_dec = [[sem(f"d_dec{i}"), 0] for i in range(4)]
        c_rel = [[sem(f"d_rel{i}"), 0] for i in range(4)]
        c_raw = [[sem(f"d_raw{i}"), 0] for i in range(NRAW)]
        IDENT, ONE = COM[:, 0:128], COM[:, 128:129]

        def par_col(name, j=0):
            c = PCOL[name] + j
            return PAR[:, c:c + 1]

        def mm(o, l, r, start, stop, *toks, inc=False):
            us = max(columns(o), 64) * (4 if r.dtype == F else 1) / 2400
            return PE.do(lambda e: e.matmul(o, l, r, start=start, stop=stop, skip_group_check=True), *toks, inc=inc,
                         us=us)

        def transpose(o, i, *toks, inc=False):
            return PE.do(lambda e: e.transpose(o, i, IDENT), *toks, inc=inc, us=0.2)

        def act(o, i, f, *toks, bias=None, scale=None, accum=None):
            kw = {}
            if bias is not None:
                kw["bias"] = bias
            if scale is not None:
                kw["scale"] = scale
            if accum is not None:
                kw["accum_out"] = accum
            us = 0.1 + columns(o) * 0.00083
            if f in OWN_TABLE and f is not A.set:
                A.set, us = f, us + 1.28
            return A.do(lambda e: e.activation(o, i, f, **kw), *toks, us=us)

        def tt(o, a, b, op, *toks, q=None):
            us = 0.06 + columns(o) * (0.17 if op is ALU.pow else 0.0022 if q is G else 0.00055 if o.dtype == B16 else 0.00105)
            return (q or V).do(lambda e: e.tensor_tensor(o, a, b, op), *toks, us=us)

        def ts(o, a, s1, s2, op0, op1, *toks):
            if op1 is None:
                return V.do(lambda e: e.tensor_scalar(o, a, s1, None, op0), *toks, us=0.06 + columns(o) * 0.0007)
            return V.do(lambda e: e.tensor_scalar(o, a, s1, s2, op0, op1), *toks, us=0.06 + columns(o) * 0.0007)

        def stt(o, a, s, b, op0, op1, *toks, q=None):
            return (q or V).do(lambda e: e.scalar_tensor_tensor(out=o, in0=a, scalar=s, in1=b, op0=op0, op1=op1), *toks,
                               us=0.06 + columns(o) * (0.0025 if q is G else 0.00105))

        def vcopy(o, a, *toks):
            return V.do(lambda e: e.tensor_copy(o, a), *toks, us=0.06 + columns(o) * 0.0007)

        def reduce_(o, i, op, *toks):
            return V.do(lambda e: e.tensor_reduce(o, i, AX, op), *toks, us=0.06 + columns(i) * 0.00105)

        def split(src, hi, lo, ready, *frees, q=None):
            th = act(hi, src, ACT.Copy, ready, *frees)
            return tt(lo, src, hi.bitcast(F), ALU.subtract, th, ready, *frees, q=q)

        class Weights:
            def __init__(self):
                self.loaded = self.splitted = 0
                self.order = []
                self.pending = 0
                self.on_pool = 0
                self.raw_free = [None] * NRAW
                self.free = [None] * NSPLIT
                self.raw_tok, self.tok = {}, {}

            def load(self):
                b = self.loaded
                if b >= N_BLOCKS:
                    return
                s = b % NRAW
                self.raw_tok[b] = S.dma(lambda e: e.dma_start(RAW[:, s, :], wall[b]), c_raw[s], self.raw_free[s])
                self.loaded += 1

            def split(self):
                b = self.splitted
                if b >= N_BLOCKS:
                    return
                r, s = b % NRAW, b % NSPLIT
                q = G if self.on_pool and b % self.on_pool == 0 else V
                self.tok[b] = split(RAW[:, r, :], WH[:, s, :], WL[:, s, :], self.raw_tok[b], self.free[s], q=q)
                self.raw_free[r] = self.tok[b]
                self.splitted += 1
                self.load()

            def take(self, *name):
                b = len(self.order)
                if b not in self.tok:
                    self.pump()
                self.order.append(name)
                s = b % NSPLIT
                return WH[:, s, :], WL[:, s, :], self.tok[b]

            def done(self, tok):
                self.pump()
                self.free[(len(self.order) - 1) % NSPLIT] = tok
                self.pending = 1

            def pump(self):
                if self.pending:
                    self.pending = 0
                    self.split()

        W = Weights()
        tasks = Tasks(PE, (V, A))

        def until(done):
            while not done():
                tasks.step()

        def half_way():
            W.pump()
            tasks.tick()

        def mm3(o, lh, ll, rh, rl, first, last, *toks, inc=False):
            mm(o, lh, rh, first, False, *toks)
            mm(o, lh, rl, False, False)
            return mm(o, ll, rh, False, last, inc=inc)

        def c128(i):
            return slice(128 * i, 128 * i + 128)

        def project_t(pool, nk, wtile, lhs_tok, hi, lo, h_tok):
            bank = pool.get()
            for k in range(nk):
                wh, wl = wtile(k)
                tok = mm3(bank.t[:, 0:T], wh, wl, hi[:, k, :], lo[:, k, :], k == 0, k == nk - 1,
                          lhs_tok, h_tok[k], bank.free, inc=(k == nk - 1))
                if nk == KD and k == 3:
                    half_way()
                elif nk == KD and k in (1, 5):
                    tasks.tick()
            return bank, tok

        ahead, sqn_free = {}, [None]

        def project_block(pool, name, idx, hi, lo, h_tok):
            if (name, idx) in ahead:
                return ahead.pop((name, idx))
            while not pool.has():
                tasks.step()
            wh, wl, wt = W.take(name, idx)
            bank, tok = project_t(pool, KD, lambda k: (wh[:, c128(k)], wl[:, c128(k)]), wt, hi, lo, h_tok)
            W.done(tok)
            return bank, tok

        def project_natural(pool, name, dst, ncols, h_tok, parts=None):
            for c in range(ncols // 512):
                b2 = [pool.get(), pool.get()]
                for kb in range(4):
                    wh, wl, wt = W.take(name, 4 * c + kb)
                    for t_ in range(2):
                        for k2 in range(2):
                            k = 2 * kb + k2
                            tok = mm3(b2[t_].t[:, :], HH[:, k, c128(t_)], HL[:, k, c128(t_)],
                                      wh[:, 512 * k2:512 * k2 + 512], wl[:, 512 * k2:512 * k2 + 512],
                                      k == 0, k == KD - 1, wt, h_tok[k], b2[t_].free, inc=True)
                        if t_ == 0:
                            half_way()
                    W.done(tok)
                    tasks.tick()
                for t_ in range(2):
                    last = act(dst[:, t_, 512 * c:512 * c + 512], b2[t_].t[:, :], ACT.Identity, tok,
                               scale=SM[0][:, t_:t_ + 1])
                    pool.put(b2[t_], last)
                if parts is not None:
                    parts[c] = last
            return last

        def acc_view(m):
            return banks[m // 2].t[:, (m % 2) * T:(m % 2) * T + T]

        def accumulate(name, idx, xh, xl, x_tok, first, last):
            wh, wl, wt = W.take(name, idx)
            toks = []
            for m in range(KD):
                tok = mm3(acc_view(m), wh[:, c128(m)], wl[:, c128(m)], xh, xl, first and m % 2 == 0, last,
                          wt, x_tok, banks[m // 2].free if first else None, inc=(m == KD - 1 or last and m % 2 == 1))
                if m % 2 == 1:
                    toks.append(tok)
                if m == 3:
                    half_way()
                elif m in (1, 5):
                    tasks.tick()
            W.done(tok)
            return toks if last else tok

        def look_ahead(names, at):
            for i, (name, idx) in enumerate(names):
                ahead[name, idx] = project_block(Pool([banks[4 + at + i]]), name, idx, HH, HL, h_tok)

        def move_on(nxt, h_free, sums=None, squares=None):
            lasts = [q.last for q in (PE, V, A, G)]
            high, sq_tok = {}, {}

            def low(m):
                gain = par_col(nxt[0], m)
                h_tok[m] = stt(HL[:, m, :], XT[:, m, :], gain, HH[:, m, :].bitcast(F), ALU.mult, ALU.subtract, high[m])

            for m in range(KD):
                if sums is not None:
                    x_tok[m] = tt(XT[:, m, :], XT[:, m, :], acc_view(m), ALU.add, sums[m // 2], x_tok[m])
                    banks[m // 2].free = x_tok[m]
                if nxt is not None:
                    high[m] = act(HH[:, m, :], XT[:, m, :], ACT.Identity, x_tok[m], h_free, scale=par_col(nxt[0], m))
                    if m:
                        low(m - 1)
            if nxt is not None:
                low(KD - 1)
                for m in range(KD):
                    sq_tok[m] = squares[m] if squares else act(SQN[:, m, :], XT[:, m, :], ACT.Square, x_tok[m],
                                                               sqn_free[0])
                for m in range(1, KD):
                    sq_tok[m] = tt(SQN[:, 0, :], SQN[:, 0, :], SQN[:, m, :], ALU.add, sq_tok[m], sq_tok[m - 1])
                look_ahead(nxt[1:3], 0)
                b1, b2 = (banks[7], banks[7]) if nxt is phases[4] else (banks[0], banks[1])
                V.wait(lasts)
                tok = norm_factor(sq_tok, b1, b2, lambda: look_ahead(nxt[3:], 2))
                b2.free = vcopy(RN[:, :], b2.t[:, 0:T], tok)
                lasts.append(b2.free)
            for q in (V, A, G):
                q.wait(lasts)
            for q in (PE, S):
                q.wait(lasts[:4])

        def inverse_root(sums, n, tmp, tok):
            r, ms, y = tmp
            free = ts(ms, sums, 1.0 / n, EPS, ALU.mult, ALU.add, tok, V.last)
            half = NHALF[:, :, 0:sums.shape[2]] if len(sums.shape) == 3 else NHALF[:, 0, 0:2]
            tp = tt(r, ms, half, ALU.pow, free, q=G)
            V.wait(tp)
            tt(y, r, r, ALU.mult, V.last)
            tt(y, y, ms, ALU.mult, V.last)
            ts(y, y, -0.5, 1.5, ALU.mult, ALU.add, V.last)
            return tt(r, r, y, ALU.mult, V.last), free

        def norm_factor(sq_tok, b1, b2, between=lambda: None):
            for i in range(2):
                tok = mm(b1.t[:, i:i + 1], SQN[:, 0, c128(i)], ONE, True, True, sq_tok[KD - 1], b1.free, inc=True)
            sqn_free[0] = tok
            tr, b1.free = inverse_root(b1.t[:, 0:2], D, [x[:, :] for x in SM], tok)
            between()
            for i in range(2):
                tok = mm(b2.t[:, c128(i)], SM[0][:, i:i + 1].to_broadcast([128, 128]), IDENT, True, True,
                         tr, b2.free, inc=(i == 1))
            return tok

        x_tok, h_tok = [None] * KD, [None] * KD
        for k in range(4):
            two = slice(2 * k, 2 * k + 2)
            x_tok[2 * k] = x_tok[2 * k + 1] = S.dma(lambda e, two=two: e.dma_start(XT[:, two, :], xt[:, two, :]), c_x[k])
        t_par = S.dma(lambda e: e.dma_start(PAR[:, :], par), c_par)
        t_con = S.dma(lambda e: e.dma_start(COM[:, :], con[:, 0:NCOMMON]), c_con)
        t_half = G.do(lambda e: e.memset(NHALF[:, :, :], -0.5))
        G.wait(t_half)
        t_one = G.do(lambda e: e.memset(ONEC[:, :], 1.0))
        t_par = [t_par, t_con, t_one]

        def constant(name, ph, rows=128, chan=c_late):
            o, n = CCOL[name]
            t = sb("c_" + name + str(S.count + len(S.items)), [128, n], F, ph)
            return t[0:rows, :], S.dma(lambda e: e.dma_start(t[0:rows, :], con[0:rows, o:o + n]), chan)

        phases = [("ffn_norm0", ("gate0", 0), ("val0", 0), ("gate0", 1)),
                  ("mix_norm1", ("qk", 0), ("qk", 8), ("qk", 1)),
                  ("ffn_norm1", ("gate1", 0), ("val1", 0), ("gate1", 1)),
                  ("norm_attn_2", ("sqk", 0), ("sqk", 4), ("sqk", 1)),
                  ("norm_ffn_2", ("pq", 0), ("pq", 1), ("pq", 2))]

        early = ExitStack()
        SQN = sb("SQN", [128, KD, T], F, early)

        with ExitStack() as ph:
            INV, t_inv = constant("invcnt", ph)
            for _ in range(NRAW):
                W.load()
            PAD = T + 16
            H0 = sb("H0", [128, KD, PAD], F, ph)
            PA, PB = sb("PA", [128, KD, PAD], F, ph), sb("PB", [128, KD, PAD], F, ph)
            Y = sb("Y", [128, KD, T], F, ph)
            t_z = G.do(lambda e: e.memset(H0[:, :, 0:16], 0.0))
            sq_tok, n_tok = {}, {}
            for m in range(KD):
                sq_tok[m] = act(SQN[:, m, :], XT[:, m, :], ACT.Square, x_tok[m])
                if m:
                    sq_tok[m] = tt(SQN[:, 0, :], SQN[:, 0, :], SQN[:, m, :], ALU.add, sq_tok[m], sq_tok[m - 1])
            for q in (PE, V, A):
                q.wait(t_par)
            tok = norm_factor(sq_tok, banks[4], banks[5])
            for m in (6, 7, 0, 1, 2, 3, 4, 5):
                n_tok[m] = banks[5].free = stt(H0[:, m, 16:PAD], XT[:, m, :], par_col("mix_norm0", m),
                                               banks[5].t[:, 0:T], ALU.mult, ALU.mult, tok)
            W.split()
            sums, p_tok, y_tok = {}, {}, {}
            for g in (3, 0, 1, 2):
                q = G if g == 3 else V
                two = slice(2 * g, 2 * g + 2)
                src, t = H0[:, two, :], [n_tok[2 * g + 1], t_z]
                for step in range(g + 1):
                    sh = 1 << step
                    at = 2 * sh - 1
                    dst = (PA, PB)[step % 2][:, two, :]
                    t = tt(dst[:, :, at:PAD], src[:, :, at:PAD], src[:, :, at - sh:PAD - sh], ALU.add, t, q=q)
                    src = dst
                sums[g] = src, t
            for g in range(4):
                (src, t), w, two = sums[g], 2 << g, slice(2 * g, 2 * g + 2)
                t1 = stt(Y[:, two, :], src[:, :, 16:PAD], 1.0 / w, H0[:, two, 16:PAD], ALU.mult, ALU.subtract, t)
                inv = INV[:, 16 * g:16 * g + w - 1].unsqueeze(1).to_broadcast([128, 2, w - 1])
                t1 = tt(Y[:, two, 0:w - 1], src[:, :, 16:15 + w], inv, ALU.mult, t1, t_inv)
                y_tok[g] = tt(Y[:, two, 0:w - 1], Y[:, two, 0:w - 1], H0[:, two, 16:15 + w], ALU.subtract, t1)
                if g:
                    two = slice(2 * g - 2, 2 * g)
                    p_tok[g - 1] = split(Y[:, two, :], HH[:, two, :], HL[:, two, :], y_tok[g - 1])
            p_tok[3] = split(Y[:, 6:8, :], HH[:, 6:8, :], HL[:, 6:8, :], y_tok[3])
            W.split()
            W.split()
            BS = sb("BS", [128, 8], F, ph)
            at_b, at_s = PCOL["pool_b"], PCOL["pool_scale"]
            t_bs = tt(BS[:, :], PAR[:, at_b:at_b + 8], PAR[:, at_s:at_s + 8], ALU.mult, q=G)
            b4 = Pool(banks[4:8])
            for half in range(2):
                wh, wl, wt = W.take("pool", half)
                for g2 in range(2):
                    g = 2 * half + g2
                    for mo in range(2):
                        def wtile(k, base=512 * g2 + 128 * mo):
                            return wh[:, base + 256 * k:base + 256 * k + 128], wl[:, base + 256 * k:base + 256 * k + 128]
                        bank, tok = project_t(b4, 2, wtile, wt, HH[:, 2 * g:2 * g + 2, :], HL[:, 2 * g:2 * g + 2, :],
                                              [p_tok[g]] * 2)
                        m = 2 * g + mo
                        t = act(Y[:, m, :], bank.t[:, 0:T], ACT.Identity, tok, p_tok[g], t_bs,
                                bias=BS[:, m:m + 1], scale=par_col("pool_scale", m))
                        b4.put(bank, t)
                        x_tok[m] = tt(XT[:, m, :], XT[:, m, :], Y[:, m, :], ALU.add, t)
                W.done(tok)
            for m in range(KD):
                sq_tok[m] = act(SQN[:, m, :], XT[:, m, :], ACT.Square, x_tok[m], sqn_free[0])
            move_on(phases[0] if upto >= 1 else None, PE.last, squares=sq_tok)

        def ffn(i):
            with ExitStack() as ph:
                tasks.slack, tasks.lead = AHEAD_F
                main = Pool(banks[7:8])
                GB_, C, SI, GG = (sb(f"{n}{i}", [128, 2, T], F, ph) for n in ("GB", "C", "SI", "GG"))
                g_tok, acc_tok = [None] * JF, [None] * JF

                def out_block(j):
                    acc_tok[j] = accumulate(f"out{i}", j, GH[:, j % 2, :], GL[:, j % 2, :], g_tok[j], j == 0, j == JF - 1)

                val = {}

                def chain(j, gb, g_pe):
                    s = j % 2
                    before = g_tok[j - 2] if j >= 2 else None
                    cw = [par_col(f"conv{i}", 22 * t + j) for t in range(3)]
                    yield
                    v0 = tt(GB_[:, s, :], gb.t[:, 0:T], RN[:, :], ALU.mult, g_pe, before)
                    main.put(gb, v0)
                    a1 = act(C[:, s, :], GB_[:, s, :], ACT.Identity, v0, before,
                             bias=par_col(f"conv_b{i}", j), scale=cw[2])
                    yield
                    v1 = stt(C[:, s, 1:T], GB_[:, s, 0:T - 1], cw[1], C[:, s, 1:T], ALU.mult, ALU.add, a1)
                    v2 = stt(C[:, s, 2:T], GB_[:, s, 0:T - 2], cw[0], C[:, s, 2:T], ALU.mult, ALU.add, v1)
                    yield
                    a2 = act(SI[:, s, :], C[:, s, :], ACT.Silu, v2)
                    a2 = tt(SI[:, s, :], SI[:, s, :], RN[:, :], ALU.mult, a2, q=G)
                    yield
                    while j not in val:
                        yield
                    vb, v_pe = val[j]
                    v3 = tt(GG[:, s, :], SI[:, s, :], vb.t[:, 0:T], ALU.mult, a2, v_pe)
                    main.put(vb, v3)
                    yield
                    g_tok[j] = split(GG[:, s, :], GH[:, s, :], GL[:, s, :], v3, acc_tok[j - 2] if j >= 2 else None)

                tasks.add(chain(0, *project_block(main, f"gate{i}", 0, HH, HL, h_tok)))
                for j in range(JF):
                    tasks.tick()
                    val[j] = project_block(main, f"val{i}", j, HH, HL, h_tok)
                    tasks.tick()
                    if j < JF - 1:
                        tasks.add(chain(j + 1, *project_block(main, f"gate{i}", j + 1, HH, HL, h_tok)))
                        tasks.tick()
                    h_free = PE.last
                    if j:
                        until(lambda: g_tok[j - 1] is not None)
                        out_block(j - 1)
                tasks.drain()
                out_block(JF - 1)
                move_on(phases[2 * i + 1] if upto >= 2 * i + 2 else None, h_free, acc_tok[JF - 1])

        def head_rows(a):
            return slice(64 * a, 64 * a + 64)

        def small_sets(ph, name):
            return [([sb(f"{name}{k}{i}", [128, 2, 8], F, ph) for i in range(3)], sb(f"{name}T{k}", [8, T], F, ph))
                    for k in range(2)]

        small_use = [0]

        def norm_steps(pool, sqs, blk, sel, n, sets, fin, read=None):
            cpc = blk.shape[1]
            w = cpc * len(sqs)
            (small, rt), small_use[0] = sets[small_use[0] % 2], small_use[0] + 1
            while not pool.has():
                yield
            bank = pool.get()
            for i, (sq, t) in enumerate(sqs):
                for k in range(2):
                    tok = mm(bank.t[:, 8 * k + cpc * i:8 * k + cpc * i + cpc], sq[:, c128(k)], blk, True, True,
                             t, bank.free, inc=True)
            if read is not None:
                read(tok)
            yield
            sums = bank.t[:, 0:16].rearrange("p (k c) -> p k c", k=2)[:, :, 0:w]
            tr, free = inverse_root(sums, n, [x[:, :, 0:w] for x in small], tok)
            pool.put(bank, free)
            yield
            while not pool.has():
                yield
            bank = pool.get()
            for k in range(2):
                tok = transpose(bank.t[0:w, c128(k)], small[0][:, k, 0:w], tr, bank.free, inc=(k == 1))
            yield
            tr = vcopy(rt[0:w, :], bank.t[0:w, 0:T], tok, PE.last)
            pool.put(bank, tr)
            yield
            for i0 in range(0, len(sqs), 2):
                while not pool.has():
                    yield
                bank = pool.get()
                mine = range(i0, min(i0 + 2, len(sqs)))
                for i in mine:
                    tok = mm(bank.t[:, T * (i - i0):T * (i - i0) + T], sel[0:w, c128(i)], rt[0:w, :], True, True,
                             tr, bank.free, inc=True)
                yield
                for i in mine:
                    free = fin(i, bank.t[:, T * (i - i0):T * (i - i0) + T], tok)
                pool.put(bank, free)
            yield

        def take_chunk(main, name, idx, dst, sq, h_tok, sq_free):
            bank, tok = project_block(main, name, idx, HH, HL, h_tok)
            t = tt(dst, bank.t[:, 0:T], RN[:, :], ALU.mult, tok)
            main.put(bank, t)
            return tt(sq, dst, dst, ALU.mult, t, sq_free, q=G), t

        def start_acc(bg):
            kept = Pool([])
            while len(kept.banks) < 4:
                for b in list(bg.banks):
                    if b in banks[0:4]:
                        bg.banks.remove(b)
                        kept.banks.append(b)
                if len(kept.banks) < 4:
                    tasks.step()

        def attention():
            ph = ExitStack()
            tasks.slack, tasks.lead = AHEAD_A
            B = sb("B", [128, 16, 384], F, ph)
            BLK2, _ = constant("blk2", ph)
            SEL2, t_c = constant("sel2", ph, 8)
            t_b, t_m = {}, {}

            def load_bias(g):
                four = slice(4 * g, 4 * g + 4)
                t_b[g] = S.dma(lambda e: e.dma_start(B[:, four, :], rel[:, four, :]), c_rel[g])

            def mask_bias(g):
                four = slice(4 * g, 4 * g + 4)
                V.do(lambda e: e.memset(B[0:64, four, 64:128], -1e30), t_b[g])
                t_m[g] = V.do(lambda e: e.memset(B[0:64, four, 320:384], -1e30))
            Q, K = sb("Q", [128, KD, T], F, ph), sb("K", [128, KD, T], F, ph)
            VN = sb("VN", [128, 2, D], F, ph)
            SS = sb("SS", [128, 16, 384], F, ph)
            SQG = sb("SQG", [128, 4, T], F, ph)
            PT = sb("PT", [128, 16, 384], F, ph)
            AH, AL = sb("AH", [128, KD, T], R, ph), sb("AL", [128, KD, T], R, ph)
            MX, NM, SE, RC = (sb(n, [128, 32], F, ph) for n in ("MX", "NM", "SE", "RC"))
            sets = small_sets(ph, "sa")
            main, bg = Pool(banks[7:8]), Pool(banks[0:4])
            W.on_pool = 3
            v_tok = {}
            a_tok, sq_free = [None] * KD, [None]
            spans = ((0, 128), (128, 384))

            def pair(m, qk_tok):
                heads = (2 * m, 2 * m + 1)
                while not bg.has(2):
                    yield
                if m // 2 not in t_m:
                    mask_bias(m // 2)
                two = [bg.get(), bg.get()]
                toks = []
                for a, h in enumerate(heads):
                    b, r = two[a], head_rows(a)
                    mm(b.t[:, 0:128], Q[r, m, 0:128], K[r, m, 0:128], True, True, b.free, qk_tok)
                    toks.append(mm(b.t[:, 128:384], Q[r, m, 128:256], K[r, m, :], True, True, inc=True))
                yield
                for a, h in enumerate(heads):
                    t = stt(SS[:, h, :], two[a].t[:, 0:384], 0.125, B[:, h, :], ALU.mult, ALU.add, toks[a], t_m[m // 2])
                    bg.put(two[a], t)
                yield
                for i, (lo, hi) in enumerate(spans):
                    reduce_(MX[:, 4 * m + 2 * i:4 * m + 2 * i + 2], SS[:, 2 * m:2 * m + 2, lo:hi], ALU.max, t)
                t = ts(NM[:, 4 * m:4 * m + 4], MX[:, 4 * m:4 * m + 4], -1.0, None, ALU.mult, None, V.last)
                yield
                for i, (lo, hi) in enumerate(spans):
                    for a, h in enumerate(heads):
                        c = 4 * m + 2 * i + a
                        te = act(SS[:, h, lo:hi], SS[:, h, lo:hi], ACT.Exp, t, bias=NM[:, c:c + 1], accum=SE[:, c:c + 1])
                yield
                t = V.do(lambda e: e.reciprocal(RC[:, 4 * m:4 * m + 4], SE[:, 4 * m:4 * m + 4]), te)
                for i, (lo, hi) in enumerate(spans):
                    for a, h in enumerate(heads):
                        c = 4 * m + 2 * i + a
                        tn = ts(SS[:, h, lo:hi], SS[:, h, lo:hi], RC[:, c:c + 1], None, ALU.mult, None, t)
                yield
                while not bg.has(2):
                    yield
                two = [bg.get(), bg.get()]
                for a, h in enumerate(heads):
                    for i in range(3):
                        toks[a] = transpose(two[a].t[:, c128(i)], SS[:, h, c128(i)], tn, two[a].free, inc=(i == 2))
                yield
                for a, h in enumerate(heads):
                    tp = act(PT[:, h, :], two[a].t[:, 0:384], ACT.Copy, toks[a])
                    bg.put(two[a], tp)
                yield
                while not bg.has() or m // 4 not in v_tok:
                    yield
                ob = bg.get()
                for a, h in enumerate(heads):
                    r, p = head_rows(a), PT[:, h, :]
                    mm(ob.t[r, 0:T], VN[:, 0, 64 * h:64 * h + 64], p[:, 0:T], True, False, tp, v_tok[m // 4], ob.free)
                    tok = mm(ob.t[r, 128:T], VN[:, 1, 64 * h:64 * h + 64], p[:, T:384], False, True, inc=True)
                yield
                th = act(AH[:, m, :], ob.t[:, 0:T], ACT.Copy, tok)
                a_tok[m] = tt(AL[:, m, :], ob.t[:, 0:T], AH[:, m, :].bitcast(F), ALU.subtract, th)
                bg.put(ob, a_tok[m])

            def group(g, sqs, dsts):
                def fin(i, root, tok):
                    gain = "attn_q_norm" if i % 2 == 0 else "attn_k_norm"
                    t = stt(dsts[i], dsts[i], par_col(gain), root, ALU.mult, ALU.mult, tok)
                    if i % 2 == 1:
                        tasks.add(pair(2 * g + i // 2, t))
                    return t
                PE.wait(t_c)
                yield from norm_steps(bg, sqs, BLK2, SEL2, 64, sets, fin, sq_free.append)

            for g in range(4):
                sqs, dsts = [], []
                until(lambda: len(sq_free) > g)
                for i in range(4):
                    m = 2 * g + i // 2
                    dst = (Q, K)[i % 2][:, m, :]
                    if i == 1:
                        load_bias(g)
                    t, tc = take_chunk(main, "qk", 8 * (i % 2) + m, dst, SQG[:, i, :], h_tok, sq_free[g])
                    sqs.append((SQG[:, i, :], [t, tc]))
                    dsts.append(dst)
                    if i < 3:
                        tasks.tick()
                tasks.add(group(g, sqs, dsts))
                tasks.tick()
            project_natural(main, "v", VN, D, h_tok, v_tok)
            bg.banks += main.banks
            start_acc(bg)
            for m in range(KD):
                until(lambda: a_tok[m] is not None)
                h_free = PE.last
                tok = accumulate("wo", m, AH[:, m, :], AL[:, m, :], a_tok[m], m == 0, m == KD - 1)
                tasks.tick()
            tasks.drain()
            W.on_pool = 0
            move_on(phases[2] if upto >= 3 else None, h_free, tok)
            ph.close()

        def mixers():
            ph = ExitStack()
            tasks.slack, tasks.lead = AHEAD_M
            (BLK2, _), (SEL2, t_c) = constant("blk2", ph), constant("sel2", ph, 8)
            (NMASK, _), (TRI, _), (ONES, _), (ROT, _), (CS, _), (SN, _), (CEN, _) = (
                constant(n, ph, chan=c_mid) for n in ("nmask", "tri", "ones", "rot", "cos", "sin", "cen"))
            SEL1, t_c2 = constant("sel1", ph, 8, chan=c_mid)
            DECF = sb("DEC", [128, 3072], F, ph)[:, :]
            t_dec = []

            def load_decay(g):
                o, cols = CCOL["decay"][0], slice(768 * g, 768 * g + 768)
                t_dec.append(S.dma(lambda e: e.dma_start(DECF[:, cols], con[:, o + cols.start:o + cols.stop]), c_dec[g]))

            DEC = DECF.rearrange("p (h c) -> p h c", h=8)
            RQ, RK, SQ_, SK = (sb(n, [128, 4, T], F, ph) for n in ("RQ", "RK", "SQ_", "SK"))
            RV, SV = sb("RV", [128, 2, D], F, ph), sb("SV", [128, 2, 512], F, ph)
            RG, GA, GB = (sb(n, [128, KD, T], F, ph) for n in ("RG", "GA", "GB"))
            SBH, SBL = sb("SBH", [128, 4, T], R, ph), sb("SBL", [128, 4, T], R, ph)
            RTH, RTL = sb("RTH", [128, KD, T], R, ph), sb("RTL", [128, KD, T], R, ph)
            ZS, LS, NS_ = (sb(n, [128, 2, 768], F, ph) for n in ("ZS", "LS", "NS_"))
            SQG = sb("SQG2", [128, 4, T], F, ph)
            RP = sb("RP", [128, 2, T], F, ph)
            sets = small_sets(ph, "sm")
            main, bg = Pool(banks[7:8]), Pool(banks[0:4])
            done = {"stick": 0, "ret": 0, "rg": None}
            slot_free = [None, None]
            sq_free = [None]
            rt_tok = [None] * 8
            sb_tok = [None] * 4

            def stick(m, qk_tok, sv_tok):
                s = m % 2
                Z, L, N = (x[:, s, :] for x in (ZS, LS, NS_))
                Z2, L2, N2 = (x.rearrange("p (a c) -> p a c", a=2) for x in (Z, L, N))
                NM2 = NMASK.unsqueeze(1).to_broadcast([128, 2, 384])
                while not bg.has(2) or (m >= 2 and sb_tok[m - 2] is None):
                    yield
                for q in (PE, V):
                    q.wait(t_c2)
                two, toks = [bg.get(), bg.get()], [None, None]
                for a in range(2):
                    b, r = two[a], head_rows(a)
                    mm(b.t[:, 0:T], SK[r, m, 0:128], SQ_[r, m, :], True, True, b.free, qk_tok)
                    toks[a] = mm(b.t[:, T:384], SK[r, m, 128:T], SQ_[r, m, 128:T], True, True, inc=True)
                yield
                for a in range(2):
                    t = act(Z2[:, a, :], two[a].t[:, 0:384], ACT.Copy, toks[a], slot_free[s], scale=0.125)
                    bg.put(two[a], t)
                yield
                t = act(L, Z, ACT.Abs, t)
                t = act(L, L, ACT.Exp, t, scale=-1.0)
                t = act(L, L, ACT.Ln, t, bias=ONEC[:, :])
                yield
                stt(N, Z, 0.0, L, ALU.max, ALU.add, t, slot_free[s])
                tn = tt(N2, N2, NM2, ALU.mult, V.last)
                yield
                tz = stt(Z, Z, 0.0, L, ALU.min, ALU.subtract, tn)
                while not bg.has(2):
                    yield
                two = [bg.get(), bg.get()]
                for a in range(2):
                    b = two[a]
                    mm(b.t[:, 0:T], TRI, N2[:, a, 0:T], True, False, b.free, tn)
                    mm(b.t[:, 128:T], ONES, N2[:, a, T:384], False, False)
                    toks[a] = mm(b.t[:, T:384], TRI, N2[:, a, T:384], False, True, inc=True)
                yield
                for a in range(2):
                    t = tt(Z2[:, a, :], Z2[:, a, :], two[a].t[:, 0:384], ALU.add, toks[a], tz)
                    bg.put(two[a], t)
                yield
                t = act(L, Z, ACT.Exp, t)
                yield
                t = stt(L2, L2, -1.0, NM2, ALU.mult, ALU.mult, t)
                yield
                while not bg.has() or sv_tok not in v_toks:
                    yield
                ob = bg.get()
                for a in range(2):
                    h, r = 2 * m + a, head_rows(a)
                    mm(ob.t[r, 0:T], SV[:, 0, 64 * h:64 * h + 64], L2[:, a, 0:T], True, False, t, v_toks[sv_tok], ob.free)
                    tok = mm(ob.t[r, 128:T], SV[:, 1, 64 * h:64 * h + 64], L2[:, a, T:384], False, True, inc=True)
                slot_free[s] = tok
                yield
                th = act(SBH[:, m, :], ob.t[:, 0:T], ACT.Copy, tok)
                sb_tok[m] = tt(SBL[:, m, :], ob.t[:, 0:T], SBH[:, m, :].bitcast(F), ALU.subtract, th)
                bg.put(ob, sb_tok[m])
                done["stick"] += 1

            def retention(m, qk_tok, rv_tok):
                s = m % 2
                ST, Y, YQ = ZS[:, s, :], LS[:, s, 0:512], NS_[:, s, 0:512]
                ST2, Y2, YQ2 = ST.rearrange("p (a c) -> p a c", a=2), Y.rearrange("p (a c) -> p a c", a=2), YQ.rearrange("p (a c) -> p a c", a=2)
                while not bg.has(2) or done["stick"] < 4 or len(t_dec) <= m or (m >= 2 and done["ret"] < m - 1):
                    yield
                two, toks = [bg.get(), bg.get()], [None, None]
                for a in range(2):
                    b, r = two[a], head_rows(a)
                    mm(b.t[:, 0:T], RK[r, m, 0:128], RQ[r, m, :], True, True, b.free, qk_tok)
                    toks[a] = mm(b.t[:, T:384], RK[r, m, 128:T], RQ[r, m, 128:T], True, True, inc=True)
                yield
                for a in range(2):
                    t = tt(ST2[:, a, :], two[a].t[:, 0:384], DEC[:, 2 * m + a, :], ALU.mult, toks[a], slot_free[s],
                           t_dec[m])
                    bg.put(two[a], t)
                yield
                while not bg.has() or rv_tok not in v_toks:
                    yield
                b = bg.get()
                for a in range(2):
                    h, o = 2 * m + a, T * a
                    mm(b.t[:, o:o + T], RV[:, 0, c128(h)], ST2[:, a, 0:T], True, False, t, v_toks[rv_tok], b.free)
                    tok = mm(b.t[:, o + 128:o + T], RV[:, 1, c128(h)], ST2[:, a, T:384], False, True, inc=True)
                yield
                t = act(Y, b.t[:, :], ACT.Copy, tok, slot_free[s])
                bg.put(b, t)
                yield
                while not bg.has():
                    yield
                b = bg.get()
                tok = mm(b.t[:, :], CEN, Y, True, True, t, b.free, inc=True)
                yield
                t = act(Y, b.t[:, :], ACT.Copy, tok)
                bg.put(b, t)
                t2 = tt(YQ, Y, Y, ALU.mult, t, slot_free[s], q=G)
                yield
                out_tok = {}

                def fin(i, root, tok):
                    out_tok[i] = stt(Y2[:, i, :], Y2[:, i, :], par_col("group_norm", 2 * m + i), root, ALU.mult,
                                     ALU.mult, tok)
                    return out_tok[i]
                yield from norm_steps(bg, [(YQ2[:, a, :], [t2, t]) for a in range(2)], ONE, SEL1, 128, sets, fin)
                while done["rg"] is None:
                    yield
                for a in range(2):
                    h = 2 * m + a
                    t = tt(Y2[:, a, :], Y2[:, a, :], RG[:, h, :], ALU.mult, done["rg"], out_tok[a])
                    rt_tok[h] = split(Y2[:, a, :], RTH[:, h, :], RTL[:, h, :], t)
                slot_free[s] = rt_tok[2 * m + 1]
                done["ret"] += 1

            def group(kind, g, sqs, dsts, v_tok):
                def fin(i, root, tok):
                    gain = f"{kind}_{'q' if i % 2 == 0 else 'k'}_norm"
                    t = stt(dsts[i], dsts[i], par_col(gain), root, ALU.mult, ALU.mult, tok)
                    if kind == "sb" and i % 2 == 1:
                        tasks.add(stick(2 * g + i // 2, t, v_tok))
                    return t
                PE.wait(t_c)
                yield from norm_steps(bg, sqs, BLK2, SEL2, 64, sets, fin, sq_free.append)
                if kind == "sb":
                    return
                for q in (PE, V):
                    q.wait(t_c2)
                t = V.last
                for i in range(4):
                    while not bg.has():
                        yield
                    b = bg.get()
                    tok = mm(b.t[:, 0:T], ROT, dsts[i], True, True, t, b.free, inc=True)
                    yield
                    r = RP[:, i % 2, :]
                    tr = tt(r, b.t[:, 0:T], SN, ALU.mult, tok, V.last)
                    bg.put(b, tr)
                    tt(dsts[i], dsts[i], CS, ALU.mult, tok)
                    tk = tt(dsts[i], dsts[i], r, ALU.add, V.last)
                    if i % 2 == 1:
                        tasks.add(retention(2 * g + i // 2, tk, v_tok))

            def two_groups(kind, name, dq, dk, v_tok):
                for g in range(2):
                    sqs, dsts = [], []
                    group_no = 2 * (kind == "ret") + g
                    until(lambda: len(sq_free) > group_no)
                    for i in range(4):
                        m = 2 * g + i // 2
                        dst = (dq, dk)[i % 2][:, m, :]
                        if kind == "ret" and i % 2:
                            load_decay(m)
                        t, tc = take_chunk(main, name, 4 * (i % 2) + m, dst, SQG[:, i, :], h_tok, sq_free[group_no])
                        sqs.append((SQG[:, i, :], [t, tc]))
                        dsts.append(dst)
                        if i < 3:
                            tasks.tick()
                    tasks.add(group(kind, g, sqs, dsts, v_tok))
                    tasks.tick()

            def gates(name, dst):
                for m in range(KD):
                    bank, tok = project_block(main, name, m, HH, HL, h_tok)
                    t = tt(dst[:, m, :], bank.t[:, 0:T], RN[:, :], ALU.mult, tok)
                    main.put(bank, t)
                    tasks.tick()
                return t

            v_toks = {}
            two_groups("sb", "sqk", SQ_, SK, "sv")
            v_toks["sv"] = project_natural(main, "sv", SV, 512, h_tok)
            two_groups("ret", "rqk", RQ, RK, "rv")
            v_toks["rv"] = project_natural(main, "rv", RV, D, h_tok)
            t = gates("rg", RG)
            for k in range(2):
                t = act(RG[:, 4 * k:4 * k + 4, :], RG[:, 4 * k:4 * k + 4, :], ACT.Silu, t)
            done["rg"] = t
            gates("ga", GA)
            t = gates("gb", GB)
            for k in range(2):
                act(GA[:, 4 * k:4 * k + 4, :], GA[:, 4 * k:4 * k + 4, :], ACT.Sigmoid, t)
                gb_tok = act(GB[:, 4 * k:4 * k + 4, :], GB[:, 4 * k:4 * k + 4, :], ACT.Sigmoid, t)
            until(lambda: done["stick"] == 4)
            for b in range(4):
                wh, wl, wt = W.take("sbbr", b)
                for g in range(2):
                    m = 2 * b + g

                    def wtile(k, base=512 * g):
                        return wh[:, base + 128 * k:base + 128 * k + 128], wl[:, base + 128 * k:base + 128 * k + 128]

                    bank, tok = project_t(main, 4, wtile, wt, SBH, SBL, sb_tok)
                    t = tt(GB[:, m, :], GB[:, m, :], bank.t[:, 0:T], ALU.mult, tok, gb_tok)
                    main.put(bank, t)
                W.done(tok)
                tasks.tick()
            until(lambda: done["ret"] == 4)
            tasks.drain()
            start_acc(bg)
            g_tok, acc_tok = [None] * KD, [None] * KD
            for m in range(KD):
                s = m % 2
                bank, tok = project_block(main, "rbr", m, RTH, RTL, rt_tok)
                t = tt(RP[:, s, :], GA[:, m, :], bank.t[:, 0:T], ALU.mult, tok, gb_tok, g_tok[m - 2] if m >= 2 else V.last)
                main.put(bank, t)
                t = tt(RP[:, s, :], RP[:, s, :], GB[:, m, :], ALU.add, t)
                g_tok[m] = split(RP[:, s, :], GH[:, s, :], GL[:, s, :], t, acc_tok[m - 2] if m >= 2 else None)
                if m:
                    acc_tok[m - 1] = accumulate("wout", m - 1, GH[:, 1 - s, :], GL[:, 1 - s, :], g_tok[m - 1], m == 1, False)
            h_free = PE.last
            tok = accumulate("wout", 7, GH[:, 1, :], GL[:, 1, :], g_tok[7], False, True)
            move_on(phases[4] if upto >= 5 else None, h_free, tok)
            ph.close()

        def peer():
            ph = ExitStack()
            tasks.slack, tasks.lead = AHEAD_P
            IOTA = sb("IOTA", [128, 128], F, ph)[:, :]
            BIG = sb("BIG", [128, 128 * T], F, ph)
            BIG3 = BIG[:, :].rearrange("p (c t) -> p c t", t=T)
            RB = sb("RB", [128, 5, T], B16, ph)
            IREP = sb("IREP", [128, 128, 8], B16, ph)
            GT_ = sb("GT_", [128, 2, T], F, ph)
            OX = sb("OX", [128, 1024], B16, ph)
            XB = XT[:, :, :].rearrange("p k t -> p (k t)").bitcast(B16)
            O1, O2, P1, P2 = (XB[:, 1024 * k:1024 * k + 1024].rearrange("p (i t) -> p i t", t=8) for k in range(4))
            P3 = OX[:, :].rearrange("p (i t) -> p i t", t=8)
            at = [128 * T]

            def scratch(m, n):
                at[0] -= m * n
                return BIG[:, at[0]:at[0] + m * n].rearrange("p (m n) -> p m n", n=n)

            KEY = scratch(2, 128)
            QT = scratch(16, T)
            SC_ = [scratch(16, 128), scratch(16, 128)]
            I1F, I2F, GT = (scratch(8, 16) for _ in range(3))
            S2 = scratch(1, 256)[:, 0, :]
            TV = scratch(16, 16)
            TI = scratch(16, 16).bitcast(U32)
            CV = scratch(8, 16)
            CI, AB = scratch(8, 16).bitcast(U32), scratch(8, 16).bitcast(U32)
            AF = scratch(8, 16)
            IF = scratch(16, 16)
            CAND, OH = scratch(1, 2048)[:, 0, :], scratch(1, 2048)[:, 0, :]
            SMX = scratch(1, 8)[:, 0, :]
            lowest = at[0] // T
            SC4 = CAND.rearrange("p (h a b) -> p h a b", h=8, a=16)
            OH4 = OH.rearrange("p (h a b) -> p h a b", h=8, a=16)
            for m in range(KD):
                x_pe = mm(acc_view(m), IDENT, XT[:, m, :], m % 2 == 0, False, x_tok[m], banks[m // 2].free,
                          inc=(m == KD - 1))
            for m in range(KD):
                x_tok[m] = stt(XT[:, m, :], XT[:, m, :], par_col("norm_ffn_2", m), RN[:, :], ALU.mult, ALU.mult, x_pe)
            main, bg = Pool([]), Pool(banks[7:8])
            W.on_pool = POOL_ROUTE
            s_tok = {}
            r_done = []

            def scores(q4, q_tok):
                for t_ in range(2):
                    while not bg.has():
                        yield
                    bank = bg.get()
                    for l in range(4 * q4, 4 * q4 + 4):
                        tok = mm(bank.t[:, c128(l % 4)], QT[:, l, c128(t_)], KEY[:, l % 2, :], True, True,
                                 q_tok, t_key, bank.free, inc=(l % 4 == 3))
                    yield
                    t = act(SC_[t_][:, 4 * q4:4 * q4 + 4, :], bank.t[:, :].rearrange("p (a b) -> p a b", b=128),
                            ACT.Copy, tok)
                    bg.put(bank, t)
                    s_tok[t_, q4] = t

            def top16(src, work_, vals, idx, tok):
                V.do(lambda e: e.max(vals[:, 0:8], src), tok, V.last, us=0.1 + columns(src) * 0.00105)
                V.do(lambda e: e.max_index(idx[:, 0:8], vals[:, 0:8], src), V.last, us=0.1 + columns(src) * 0.00105)
                V.do(lambda e: e.match_replace(work_, vals[:, 0:8], src, NEG), V.last, us=0.1 + columns(src) * 0.00105)
                V.do(lambda e: e.max(vals[:, 8:16], work_), V.last, us=0.1 + columns(src) * 0.00105)
                return V.do(lambda e: e.max_index(idx[:, 8:16], vals[:, 8:16], work_), V.last, us=0.1 + columns(src) * 0.00105)

            def bc(ap, axis):
                return ap.unsqueeze(axis).to_broadcast([128, 8, 16, 16])

            def route():
                V.wait(t_io)
                vcopy(IREP[:, :, :], IOTA.unsqueeze(2).to_broadcast([128, 128, 8]))
                for t_ in range(2):
                    for l in range(16):
                        while (t_, l // 4) not in s_tok:
                            yield
                        top16(SC_[t_][:, l, :], S2[:, 0:128], TV[:, l, :], TI[:, l, :], s_tok[t_, l // 4])
                        yield
                    TVh = TV.rearrange("p (h s) k -> p h s k", s=2)
                    tt(SC4, bc(TVh[:, :, 0, :], 3), bc(TVh[:, :, 1, :], 2), ALU.add, V.last)
                    yield
                    for h in range(8):
                        top16(CAND[:, 256 * h:256 * h + 256], S2, CV[:, h, :], CI[:, h, :], V.last)
                        yield
                    vcopy(IF, TI, V.last)
                    IFh = IF.rearrange("p (h s) k -> p h s k", s=2)
                    for side, dst in ((0, I1F), (1, I2F)):
                        if side == 0:
                            V.do(lambda e: e.tensor_scalar(AB, CI, 4, None, ALU.logical_shift_right), V.last)
                        else:
                            V.do(lambda e: e.tensor_scalar(AB, CI, 15, None, ALU.bitwise_and), V.last)
                        vcopy(AF, AB, V.last)
                        i16 = IOTA[:, 0:16].unsqueeze(1).unsqueeze(1).to_broadcast([128, 8, 16, 16])
                        tt(OH4, bc(AF, 3), i16, ALU.is_equal, V.last)
                        yield
                        tt(OH4, OH4, bc(IFh[:, :, side, :], 2), ALU.mult, V.last)
                        yield
                        reduce_(dst, OH4, ALU.add, V.last)
                        yield
                    t = tt(GT, CV, CV[:, :, 0:1].to_broadcast([128, 8, 16]), ALU.subtract, V.last)
                    t = act(GT, GT, ACT.Exp, t)
                    yield
                    reduce_(SMX, GT, ALU.add, t)
                    V.do(lambda e: e.reciprocal(SMX, SMX), V.last)
                    t = tt(GT, GT, SMX.unsqueeze(2).to_broadcast([128, 8, 16]), ALU.mult, V.last)
                    while not bg.has():
                        yield
                    bank = bg.get()
                    for i, src in enumerate((I1F, I2F, GT)):
                        tok = transpose(bank.t[:, c128(i)], src.rearrange("p a b -> p (a b)"), t, bank.free, inc=(i == 2))
                    yield
                    cols = c128(t_)
                    vcopy(RB[:, 0:2, cols], bank.t[:, 0:T].rearrange("p (a b) -> p a b", b=128), tok)
                    t = vcopy(GT_[:, 0, cols], bank.t[:, T:384], tok)
                    bg.put(bank, t)
                    vcopy(RB[:, 2, cols], GT_[:, 0, cols], t)
                    tt(GT_[:, 1, cols], GT_[:, 0, cols], RB[:, 2, cols], ALU.subtract, V.last)
                    vcopy(RB[:, 3, cols], GT_[:, 1, cols], V.last)
                    tt(GT_[:, 1, cols], GT_[:, 1, cols], RB[:, 3, cols], ALU.subtract, V.last)
                    r_tok[0] = vcopy(RB[:, 4, cols], GT_[:, 1, cols], V.last)
                    yield
                r_done.append(1)

            r_tok = [None]
            tokens_done = [0]
            chunks_done = [0]
            slot_tok, gelu_tok = [None], [None]

            meets = []

            def meet(k):
                q, two, toks = meets[0]
                n, lo = chunks_done[0], 8 * q + 4 * k
                src = two[k].t[:, :].rearrange("p (t c) -> p c t", t=4)
                dst = BIG3[:, :, lo:lo + 4]
                tm = tt(dst[:, 0:n, :], dst[:, 0:n, :], src[:, 0:n, :], ALU.mult, toks[k], gelu_tok[0])
                if n < 128:
                    tm = act(dst[:, n:128, :], src[:, n:128, :], ACT.Copy, tm, slot_tok[0])
                bg.put(two[k], tm)
                slot_tok[0] = tm
                tokens_done[0] = lo + 4
                if k:
                    meets.pop(0)

            def gates():
                while not r_done:
                    yield
                o_free = h_tok[KD - 1]
                for q in range(T // 8):
                    sl = slice(8 * q, 8 * q + 8)

                    def row(i):
                        return RB[:, i, sl].unsqueeze(1).to_broadcast([128, 128, 8])

                    tt(O1, row(0), IREP[:, :, :], ALU.is_equal, r_tok[0], o_free)
                    t2 = tt(O2, row(1), IREP[:, :, :], ALU.is_equal)
                    yield
                    t3 = tt(P3, O2, row(4), ALU.mult, t2, o_free, q=G)
                    for i, P in enumerate((P1, P2)):
                        t = tt(P, O2, row(2 + i), ALU.mult, t2)
                    yield
                    if meets:
                        meet(0)
                    yield
                    if meets:
                        meet(1)
                    yield
                    while not bg.has(2):
                        yield
                    two = [bg.get(), bg.get()]
                    toks = [None, None]
                    for k in range(8):
                        b = two[k // 4]
                        for i, P in enumerate((P1, P2, P3)):
                            tok = mm(b.t[:, c128(k % 4)], O1[:, :, k], P[:, :, k], i == 0 and k % 4 == 0, i == 2,
                                     t, t3, b.free, inc=(i == 2 and k % 4 == 3))
                        if k == 3:
                            toks[0] = tok
                            yield
                    toks[1] = o_free = tok
                    meets.append((q, two, toks))
                    yield
                while meets:
                    meet(0)
                    yield
                    meet(1)
                    yield

            for l in range(16):
                bank, tok = project_block(main, "pq", l, HH, HL, h_tok)
                q_tok = tt(QT[:, l, :], bank.t[:, 0:T], RN[:, :], ALU.mult, tok)
                (bg if bank is banks[6] else main).put(bank, q_tok)
                if l == 3:
                    o = CCOL["iota"][0]
                    t_io = S.dma(lambda e: e.dma_start(IOTA, con[:, o:o + 128]), c_late, banks[7].free)
                    t_key = S.dma(lambda e: e.dma_start(KEY, keys), c_key)
                    tasks.add(route())
                    tasks.add(gates())
                if l % 4 == 3:
                    tasks.live.insert(0, scores(l // 4, q_tok))
                tasks.tick()
            h_free = PE.last
            for m in range(KD):
                h_tok[m] = split(XT[:, m, :], HH[:, m, :], HL[:, m, :], x_tok[m], h_free)
            for c in range(128):
                if c == lowest and not r_done:
                    until(lambda: r_done)
                if c == lowest:
                    A.wait(V.last, PE.last)
                bank, tok = project_block(main, "u", c, HH, HL, h_tok)
                W.on_pool = POOL_PEER if r_done else POOL_ROUTE
                tasks.tick()
                n = tokens_done[0]
                if n < T:
                    t = act(BIG3[:, c, n:T], bank.t[:, n:T], ACT.Gelu_apprx_tanh, tok)
                if n:
                    tmp = GT_[:, c % 2, 0:n]
                    tg = act(tmp, bank.t[:, 0:n], ACT.Gelu_apprx_tanh, tok, gelu_free[c % 2] or V.last)
                    t = tg
                    gelu_free[c % 2] = tt(BIG3[:, c, 0:n], BIG3[:, c, 0:n], tmp, ALU.mult, tg, slot_tok[0])
                main.put(bank, t)
                gelu_tok[0] = t
                chunks_done[0] = c + 1
            tasks.drain()
            W.on_pool = 0
            t_a = [V.last, A.last, slot_tok[0]]
            acc_tok, a_split = [None] * 128, [None] * 128
            for c in range(128):
                s = c % 2
                a_split[c] = split(BIG3[:, c, :], GH[:, s, :], GL[:, s, :], t_a, acc_tok[c - 2] if c >= 2 else None)
                if c:
                    acc_tok[c - 1] = accumulate("w", c - 1, GH[:, 1 - s, :], GL[:, 1 - s, :], a_split[c - 1], False, False)
            tok = accumulate("w", 127, GH[:, 1, :], GL[:, 1, :], a_split[127], False, True)
            for m in range(KD):
                x_tok[m] = vcopy(XT[:, m, :], acc_view(m), tok)
            ph.close()

        gelu_free = [None, None]
        if upto >= 1:
            ffn(0)
        if upto >= 2:
            attention()
        if upto >= 3:
            ffn(1)
        if upto >= 4:
            mixers()
        early.close()
        if upto >= 5:
            peer()
        for c in c_raw:
            S.wait((c[0], c[1]))
        for k in range(4):
            t_o = S.dma(lambda e, k=k: e.dma_start(out[:, 2 * k:2 * k + 2, :], XT[:, 2 * k:2 * k + 2, :]), c_out,
                        x_tok[2 * k], x_tok[2 * k + 1])
        S.wait(t_o)

        block = ctx.enter_context(nc.Block())

        @block.sync
        def _(e):
            S.replay(e)

        @block.scalar
        def _(e):
            A.replay(e)

        @block.vector
        def _(e):
            V.replay(e)

        @block.gpsimd
        def _(e):
            G.replay(e)

        @block.tensor
        def _(e):
            PE.replay(e)
        return W.order


def _vec(v):
    return v.reshape(-1, 128).T


def _cols(w):
    k, n = w.shape
    return w.reshape(k // 128, 128, n // 128, 128).transpose(2, 1, 0, 3).reshape(n // 128, 128, k)


def _natural(w):
    k, n = w.shape
    return w.reshape(4, 2, 128, n // 512, 512).transpose(3, 0, 2, 1, 4).reshape(-1, 128, BLK)


def _wall(i, order):
    wi = i["w_in_2"][0]
    parts = {
        "pool": i["pool_w"][0].reshape(2, 2, 2, 128, 256).transpose(0, 3, 1, 2, 4).reshape(2, 128, BLK),
        "qk": _cols(i["attn_wqkv"][0][:, 0:2048]),
        "v": _natural(i["attn_wqkv"][0][:, 2048:3072]),
        "wo": i["attn_wo"][0].reshape(8, 128, D),
        "rqk": _cols(wi[:, 0:1024]),
        "rv": _natural(wi[:, 1024:2048]),
        "rg": _cols(wi[:, 2048:3072]),
        "sqk": _cols(wi[:, 3072:4096]),
        "sv": _natural(wi[:, 4096:4608]),
        "ga": _cols(wi[:, 4608:5632]),
        "gb": _cols(wi[:, 5632:6656]),
        "sbbr": _cols(i["w_branch_sb_2"][0]).reshape(4, 2, 128, 512).transpose(0, 2, 1, 3).reshape(4, 128, BLK),
        "rbr": _cols(i["w_branch_ret_2"][0]),
        "wout": i["w_out_2"][0].reshape(8, 128, D),
        "pq": _cols(i["peer_w_q_2"][0]),
        "u": i["peer_u_2"][0].reshape(128, 128, 8, 128).transpose(1, 3, 2, 0).reshape(128, 128, BLK),
        "w": i["peer_v_2"][0].reshape(128, 128, D).transpose(1, 0, 2),
    }
    for l in range(2):
        parts[f"gate{l}"] = _cols(i["ffn_w_gate"][l])
        parts[f"val{l}"] = _cols(i["ffn_w_val"][l])
        parts[f"out{l}"] = i["ffn_w_out"][l].reshape(JF, 128, D)
    w = np.empty((N_BLOCKS, 128, BLK), np.float32)
    for at, (name, idx) in enumerate(order):
        w[at] = parts[name][idx]
    w[len(order):] = 0.0
    return w


def _params(i):
    def two(v):
        return np.concatenate([v, v]).reshape(128, 1)

    cols = [_vec(i["mix_norm"][0]), _vec(i["mix_norm"][1]), _vec(i["ffn_norm"][0]), _vec(i["ffn_norm"][1]),
            _vec(i["pool_b"][0]), _vec(i["pool_scale"][0]), two(i["attn_q_norm"][0]), two(i["attn_k_norm"][0])]
    cols += [_vec(i["ffn_conv_w"][l].reshape(-1)) for l in range(2)]
    cols += [_vec(i["ffn_conv_b"][l]) for l in range(2)]
    cols += [_vec(i["norm_attn_2"][0]), two(i["ret_q_norm_2"][0]), two(i["ret_k_norm_2"][0]),
             _vec(i["ret_group_norm_2"][0]), two(i["sb_q_norm_2"][0]), two(i["sb_k_norm_2"][0]),
             _vec(i["norm_ffn_2"][0])]
    return np.ascontiguousarray(np.concatenate(cols, axis=1))


def _relative(table):
    q = np.arange(128)[:, None]
    at = np.concatenate([256 + q - np.arange(128)[None, :], 384 + q - np.arange(T)[None, :]], axis=1)
    return np.ascontiguousarray(table[:, at].transpose(1, 0, 2))


def _constants():
    c = np.zeros((128, NCON), np.float32)

    def put(name, v):
        o, n = CCOL[name]
        c[:, o:o + n] = v

    p = np.arange(128)
    t = np.arange(T)
    same = p[:, None] // 64 == p[None, :] // 64
    k, m = p[:, None] % 64, p[None, :] % 64
    put("ident", np.eye(128))
    put("one", 1.0)
    put("ones", 1.0)
    put("blk2", p[:, None] // 64 == np.arange(2)[None, :])
    col = np.arange(512)[None, :]
    put("sel2", p[:, None] == 2 * (col // 128) + col % 128 // 64)
    put("sel1", p[:, None] == col // 128)
    put("rot", same * (1.0 * (k == m - 32) - 1.0 * (k == m + 32)))
    put("tri", p[:, None] > p[None, :])
    put("cen", np.eye(128) - 1.0 / 128)
    put("iota", p[None, :])
    inv = np.zeros(64)
    for g in range(4):
        inv[16 * g:16 * g + 16] = 1.0 / np.minimum(np.arange(16) + 1, 2 << g)
    put("invcnt", inv[None, :])
    qpos = np.concatenate([t, t[128:]])[None, :]
    kpos = p[:, None] + np.concatenate([np.zeros(T), np.full(128, 128)])[None, :]
    diff = qpos - kpos
    put("decay", np.concatenate([np.where(diff >= 0, np.exp(np.log1p(-np.exp2(-5.0 - h)) * np.maximum(diff, 0)), 0.0)
                                 * 0.125 for h in range(8)], axis=1))
    freqs = (10000.0 ** (-np.arange(32, dtype=np.float32) / 32)).astype(np.float32)
    ang = (t[None, :].astype(np.float32) * freqs[p % 32][:, None]).astype(np.float32).astype(np.float64)
    put("cos", np.cos(ang))
    put("sin", np.sin(ang))
    put("nmask", -1.0 * (diff > 0))
    return c


def kernel(**inputs):
    import concourse.bacc as bacc
    from concourse.bass_utils import run_bass_kernel_spmd

    i = {n: np.asarray(a) for n, a in inputs.items()}
    arrays = {
        "wall": (N_BLOCKS, 128, BLK),
        "par": _params(i),
        "con": _constants(),
        "xt": np.ascontiguousarray(i["x"][0].reshape(T, KD, 128).transpose(2, 1, 0)),
        "rel": _relative(i["attn_rel_bias"][0]),
        "keys": np.ascontiguousarray(np.stack([i["peer_sub_keys_1_2"][0].T, i["peer_sub_keys_2_2"][0].T], axis=1)),
    }
    nc = bacc.Bacc("TRN2", target_bir_lowering=False, num_devices=1)
    args = [nc.dram_tensor(n, a if n == "wall" else a.shape, F, kind="ExternalInput").ap() for n, a in arrays.items()]
    out = nc.dram_tensor("out", (128, KD, T), F, kind="ExternalOutput").ap()
    order = build(nc, *args, out)
    arrays["wall"] = _wall(i, order)
    r = run_bass_kernel_spmd(nc, [arrays], core_ids=[0])
    got = r.results[0]["out"]
    return np.ascontiguousarray(got.transpose(2, 1, 0)).reshape(1, T, D)
```
